# Optimizing a Trainium2 kernel written in Bass

```python
import jax, jax.numpy as jnp
from jax import lax
import numpy as np

D_MODEL = 2048
BATCH = 1
SEQ = 512
DEPTH = 2

N_HEADS_MLA = 8
QK_NOPE_DIM = 128
QK_ROPE_DIM = 64
V_HEAD_DIM = 128
Q_LORA_RANK = 512
KV_LORA_RANK = 256
D_MLA = N_HEADS_MLA * V_HEAD_DIM
ROPE_THETA = 10000.0
Q_BLOCK = 128
POOL_WINDOWS = (2, 4, 8, 16)
N_POOL_GROUPS = 4
POOL_GROUP_DIM = 128
D_POOL = N_POOL_GROUPS * POOL_GROUP_DIM
N_CONV_HEADS = 4
CONV_HEAD_DIM = 128
D_CONV = N_CONV_HEADS * CONV_HEAD_DIM
CONV_WIDTH = 3
D_MIX = D_MLA + D_POOL + D_CONV
SPLIT_SIZES = (Q_LORA_RANK, KV_LORA_RANK, QK_ROPE_DIM, D_MLA, D_POOL, D_POOL, D_CONV, D_CONV, D_CONV, D_CONV)
D_IN_PROJ = sum(SPLIT_SIZES)
LN_EPS = 1e-5
RMS_EPS = 1e-6
DEEPNORM_ALPHA = (2 * DEPTH) ** 0.25
DEEPNORM_BETA = (8 * DEPTH) ** -0.25


def layernorm(x, g, b):
    xf = x.astype(jnp.float32)
    mu = jnp.mean(xf, axis=-1, keepdims=True)
    var = jnp.mean(jnp.square(xf - mu), axis=-1, keepdims=True)
    y = (xf - mu) * lax.rsqrt(var + LN_EPS) * g.astype(jnp.float32) + b.astype(jnp.float32)
    return y.astype(x.dtype)

def rmsnorm(x, g):
    xf = x.astype(jnp.float32)
    y = xf * lax.rsqrt(jnp.mean(jnp.square(xf), axis=-1, keepdims=True) + RMS_EPS) * g.astype(jnp.float32)
    return y.astype(x.dtype)

def apply_rope(x, cos, sin):
    half = QK_ROPE_DIM // 2
    xf = x.astype(jnp.float32)
    x1, x2 = xf[..., :half], xf[..., half:]
    return jnp.concatenate([x1 * cos - x2 * sin, x2 * cos + x1 * sin], axis=-1).astype(x.dtype)

def mla_mixer(q_lat, kv_lat, k_rope, positions, q_norm_g, kv_norm_g, w_uq, w_ukv):
    Bn, S, _ = q_lat.shape
    H = N_HEADS_MLA
    q = (rmsnorm(q_lat, q_norm_g) @ w_uq).reshape(Bn, S, H, QK_NOPE_DIM + QK_ROPE_DIM)
    q_nope, q_rope = q[..., :QK_NOPE_DIM], q[..., QK_NOPE_DIM:]
    kv = (rmsnorm(kv_lat, kv_norm_g) @ w_ukv).reshape(Bn, S, H, QK_NOPE_DIM + V_HEAD_DIM)
    k_nope, v = kv[..., :QK_NOPE_DIM], kv[..., QK_NOPE_DIM:]
    half = QK_ROPE_DIM // 2
    inv_freq = ROPE_THETA ** (-jnp.arange(half, dtype=jnp.float32) / half)
    ang = positions.astype(jnp.float32)[..., None] * inv_freq
    cos, sin = jnp.cos(ang), jnp.sin(ang)
    q_rope = apply_rope(q_rope, cos[:, :, None, :], sin[:, :, None, :])
    k_rope = apply_rope(k_rope, cos, sin)
    scale = (QK_NOPE_DIM + QK_ROPE_DIM) ** -0.5
    nb = S // Q_BLOCK
    qn_blocks = q_nope.reshape(Bn, nb, Q_BLOCK, H, QK_NOPE_DIM).transpose(1, 0, 2, 3, 4)
    qr_blocks = q_rope.reshape(Bn, nb, Q_BLOCK, H, QK_ROPE_DIM).transpose(1, 0, 2, 3, 4)
    key_idx = jnp.arange(S)

    def attend(args):
        qn, qr, blk = args
        s = (jnp.einsum('bqhd,bkhd->bhqk', qn, k_nope).astype(jnp.float32)
             + jnp.einsum('bqhr,bkr->bhqk', qr, k_rope).astype(jnp.float32)) * scale
        q_idx = blk * Q_BLOCK + jnp.arange(Q_BLOCK)
        causal = key_idx[None, :] <= q_idx[:, None]
        s = jnp.where(causal[None, None], s, -jnp.inf)
        p = jax.nn.softmax(s, axis=-1).astype(v.dtype)
        return jnp.einsum('bhqk,bkhd->bqhd', p, v)

    out = lax.map(attend, (qn_blocks, qr_blocks, jnp.arange(nb)))
    return out.transpose(1, 0, 2, 3, 4).reshape(Bn, S, D_MLA)

def pool_mixer(h, w_pool, pool_scale):
    Bn, S, _ = h.shape
    hg = h.reshape(Bn, S, N_POOL_GROUPS, POOL_GROUP_DIM).astype(jnp.float32)
    cs = jnp.cumsum(hg, axis=1)
    t1 = jnp.arange(1, S + 1, dtype=jnp.float32)
    means = []
    for g, w in enumerate(POOL_WINDOWS):
        c = cs[:, :, g]
        lag = jnp.pad(c, ((0, 0), (w, 0), (0, 0)))[:, :S]
        means.append((c - lag) / jnp.minimum(t1, float(w))[None, :, None])
    pooled = (jnp.stack(means, axis=2) - hg).astype(h.dtype)
    y = jnp.einsum('bsgc,gcd->bsgd', pooled, w_pool).reshape(Bn, S, D_POOL)
    return y * pool_scale

def conv_mixer(h, b_gate, c_gate, conv_w):
    u = c_gate * h
    y = lax.conv_general_dilated(u, conv_w[:, None, :], window_strides=(1,),
                                 padding=((CONV_WIDTH - 1, 0),),
                                 dimension_numbers=('NWC', 'WIO', 'NWC'),
                                 feature_group_count=D_CONV)
    return b_gate * y

def hybrid_layer(x, positions, w_in, q_norm_g, kv_norm_g, w_uq, w_ukv, w_pool, pool_scale,
                 conv_w, w_out, b_out, ln_g, ln_b):
    split_idx = np.cumsum(SPLIT_SIZES)[:-1].tolist()
    proj = x @ w_in
    (q_lat, kv_lat, k_rope, g_mla, p_in, g_pool, c_h, c_b, c_c, g_conv) = jnp.split(proj, split_idx, axis=-1)
    y_mla = mla_mixer(q_lat, kv_lat, k_rope, positions, q_norm_g, kv_norm_g, w_uq, w_ukv) * jax.nn.silu(g_mla)
    y_pool = pool_mixer(p_in, w_pool, pool_scale) * jax.nn.silu(g_pool)
    y_conv = conv_mixer(c_h, c_b, c_c, conv_w) * jax.nn.silu(g_conv)
    mix = jnp.concatenate([y_mla, y_pool, y_conv], axis=-1)
    out = mix @ w_out + b_out
    return layernorm(DEEPNORM_ALPHA * x + out, ln_g, ln_b)

def first_inputs(seed: int = 0) -> dict:
    key = jax.random.key(seed)
    ks = jax.random.split(key, 16)
    f32 = jnp.float32
    nrm = lambda k, shape, s: jax.random.normal(k, shape, f32) * s
    x = jax.random.normal(ks[0], (BATCH, SEQ, D_MODEL), f32)
    positions = jnp.broadcast_to(jnp.arange(SEQ, dtype=jnp.int32), (BATCH, SEQ))
    return {
        "x": x,
        "positions": positions,
        "emb_ln_g": 1.0 + nrm(ks[1], (D_MODEL,), 0.01),
        "emb_ln_b": nrm(ks[2], (D_MODEL,), 0.01),
        "w_in": nrm(ks[3], (DEPTH, D_MODEL, D_IN_PROJ), D_MODEL ** -0.5),
        "q_norm_g": 1.0 + nrm(ks[4], (DEPTH, Q_LORA_RANK), 0.01),
        "kv_norm_g": 1.0 + nrm(ks[5], (DEPTH, KV_LORA_RANK), 0.01),
        "w_uq": nrm(ks[6], (DEPTH, Q_LORA_RANK, N_HEADS_MLA * (QK_NOPE_DIM + QK_ROPE_DIM)), Q_LORA_RANK ** -0.5),
        "w_ukv": nrm(ks[7], (DEPTH, KV_LORA_RANK, N_HEADS_MLA * (QK_NOPE_DIM + V_HEAD_DIM)), KV_LORA_RANK ** -0.5),
        "w_pool": nrm(ks[8], (DEPTH, N_POOL_GROUPS, POOL_GROUP_DIM, POOL_GROUP_DIM), POOL_GROUP_DIM ** -0.5),
        "pool_scale": 1.0 + nrm(ks[9], (DEPTH, D_POOL), 0.1),
        "conv_w": nrm(ks[10], (DEPTH, CONV_WIDTH, D_CONV), CONV_WIDTH ** -0.5),
        "w_out": nrm(ks[11], (DEPTH, D_MIX, D_MODEL), DEEPNORM_BETA * D_MIX ** -0.5),
        "b_out": nrm(ks[12], (DEPTH, D_MODEL), 0.01),
        "ln_g": 1.0 + nrm(ks[13], (DEPTH, D_MODEL), 0.01),
        "ln_b": nrm(ks[14], (DEPTH, D_MODEL), 0.01),
    }

def first_block(x, positions, emb_ln_g, emb_ln_b, w_in, q_norm_g, kv_norm_g, w_uq, w_ukv, w_pool,
              pool_scale, conv_w, w_out, b_out, ln_g, ln_b):
    h = layernorm(x, emb_ln_g, emb_ln_b)
    for l in range(DEPTH):
        h = hybrid_layer(h, positions, w_in[l], q_norm_g[l], kv_norm_g[l], w_uq[l], w_ukv[l], w_pool[l],
                         pool_scale[l], conv_w[l], w_out[l], b_out[l], ln_g[l], ln_b[l])
    return h


DEPTH_2 = 1

D_MIX_2 = D_MODEL
WIDTH_A = D_MIX_2 // 2
WIDTH_B = D_MIX_2 - WIDTH_A
CHUNK = 128
HEADS_A = 8
DH_A = WIDTH_A // HEADS_A
HEADS_B = 16
DH_B = WIDTH_B // HEADS_B
EPS = 1e-6
SPLIT_SIZES_2 = (WIDTH_A, WIDTH_A, WIDTH_A, WIDTH_B, WIDTH_B, WIDTH_B, WIDTH_B, HEADS_B)
D_IN = sum(SPLIT_SIZES_2)


def _split_points(sizes):
    pts, acc = [], 0
    for s in sizes[:-1]:
        acc += s
        pts.append(acc)
    return pts

def rms_norm(x, g):
    xf = x.astype(jnp.float32)
    y = xf * lax.rsqrt(jnp.mean(xf * xf, axis=-1, keepdims=True) + EPS)
    return (y * g.astype(jnp.float32)).astype(x.dtype)

def layer_norm(x, g, b):
    xf = x.astype(jnp.float32)
    mu = jnp.mean(xf, axis=-1, keepdims=True)
    xc = xf - mu
    var = jnp.mean(xc * xc, axis=-1, keepdims=True)
    y = xc * lax.rsqrt(var + EPS) * g.astype(jnp.float32) + b.astype(jnp.float32)
    return y.astype(x.dtype)

def chunked_spatial_gating(u, v, ln_g, ln_b, w_s, b_s):
    bsz, s, _ = v.shape
    n = s // CHUNK
    v = layer_norm(v, ln_g, ln_b)
    vc = v.reshape(bsz, n, CHUNK, HEADS_A, DH_A)
    causal = jnp.tril(jnp.ones((CHUNK, CHUNK), dtype=bool))
    w = jnp.where(causal[None], w_s, jnp.zeros_like(w_s))
    mixed = jnp.einsum('hts,bnshd->bnthd', w, vc) + b_s.T[None, None, :, :, None]
    return u * mixed.reshape(bsz, s, WIDTH_A)

def forgetting_attention(q, k, v, f_logit, b_f):
    bsz, s, _ = q.shape
    nb = s // Q_BLOCK
    to_heads = lambda t: t.reshape(bsz, s, HEADS_B, DH_B).transpose(0, 2, 1, 3)
    q, k, v = to_heads(q), to_heads(k), to_heads(v)
    log_f = jax.nn.log_sigmoid(f_logit.astype(jnp.float32) + b_f.astype(jnp.float32))
    F = jnp.cumsum(log_f, axis=1).transpose(0, 2, 1)
    qb = q.reshape(bsz, HEADS_B, nb, Q_BLOCK, DH_B).transpose(2, 0, 1, 3, 4)
    Fb = F.reshape(bsz, HEADS_B, nb, Q_BLOCK).transpose(2, 0, 1, 3)
    k_pos = jnp.arange(s)
    scale = DH_B ** -0.5

    def block(args):
        qi, Fi, i = args
        q_pos = i * Q_BLOCK + jnp.arange(Q_BLOCK)
        logits = jnp.einsum('bhqd,bhkd->bhqk', qi, k).astype(jnp.float32) * scale
        logits = logits + (Fi[..., :, None] - F[..., None, :])
        logits = jnp.where(q_pos[:, None] >= k_pos[None, :], logits, -jnp.inf)
        p = jax.nn.softmax(logits, axis=-1)
        return jnp.einsum('bhqk,bhkd->bhqd', p.astype(v.dtype), v)

    out = lax.map(block, (qb, Fb, jnp.arange(nb)))
    return out.transpose(1, 0, 3, 2, 4).reshape(bsz, s, WIDTH_B)

def second_inputs(seed: int = 0) -> dict:
    key = jax.random.key(seed)
    ks = jax.random.split(key, 16)
    f32 = jnp.float32
    nrm = lambda k, shape: jax.random.normal(k, shape, dtype=f32)
    row_scale = (1.0 / jnp.sqrt(jnp.arange(1, CHUNK + 1, dtype=f32)))[None, None, :, None]
    b_f = jnp.linspace(1.0, 5.0, HEADS_B, dtype=f32)[None, :] + 0.1 * nrm(ks[11], (DEPTH_2, HEADS_B))
    return {
        "x": nrm(ks[0], (BATCH, SEQ, D_MODEL)),
        "c": nrm(ks[1], (BATCH, D_MODEL)),
        "norm_g": 1.0 + 0.1 * nrm(ks[2], (DEPTH_2, D_MODEL)),
        "w_ada": nrm(ks[3], (DEPTH_2, D_MODEL, 3 * D_MODEL)) * D_MODEL ** -0.5,
        "b_ada": 0.01 * nrm(ks[4], (DEPTH_2, 3 * D_MODEL)),
        "w_in": nrm(ks[5], (DEPTH_2, D_MODEL, D_IN)) * D_MODEL ** -0.5,
        "ln_v_g": 1.0 + 0.1 * nrm(ks[6], (DEPTH_2, WIDTH_A)),
        "ln_v_b": 0.01 * nrm(ks[7], (DEPTH_2, WIDTH_A)),
        "w_s": nrm(ks[8], (DEPTH_2, HEADS_A, CHUNK, CHUNK)) * row_scale,
        "b_s": 1.0 + 0.1 * nrm(ks[9], (DEPTH_2, HEADS_A, CHUNK)),
        "b_f": b_f,
        "w_out": nrm(ks[10], (DEPTH_2, D_MIX_2, D_MODEL)) * D_MIX_2 ** -0.5,
        "final_g": 1.0 + 0.1 * nrm(ks[12], (D_MODEL,)),
    }

def second_block(x, c, norm_g, w_ada, b_ada, w_in, ln_v_g, ln_v_b, w_s, b_s, b_f, w_out, final_g):
    cond = jax.nn.silu(c)
    pts = _split_points(SPLIT_SIZES_2)
    for l in range(DEPTH_2):
        mod = cond @ w_ada[l] + b_ada[l]
        shift, scale, gate = jnp.split(mod, 3, axis=-1)
        h = rms_norm(x, norm_g[l]) * (1.0 + scale[:, None, :]) + shift[:, None, :]
        z = h @ w_in[l]
        u_a, v_a, g_a, q_b, k_b, v_b, g_b, f_b = jnp.split(z, pts, axis=-1)
        y_a = chunked_spatial_gating(jax.nn.gelu(u_a, approximate=False),
                                     jax.nn.gelu(v_a, approximate=False),
                                     ln_v_g[l], ln_v_b[l], w_s[l], b_s[l]) * jax.nn.silu(g_a)
        y_b = forgetting_attention(q_b, k_b, v_b, f_b, b_f[l]) * jax.nn.silu(g_b)
        y = jnp.concatenate([y_a, y_b], axis=-1) @ w_out[l]
        x = x + gate[:, None, :] * y
    return rms_norm(x, final_g)


def setup_inputs(seed=0):
    out = dict(first_inputs(seed))
    for name, value in second_inputs(seed + 1).items():
        if name != "x":
            out[name + "_2"] = value
    return out


def reference(
    x, positions, emb_ln_g, emb_ln_b, w_in, q_norm_g, kv_norm_g, w_uq, w_ukv, w_pool,
    pool_scale, conv_w, w_out, b_out, ln_g, ln_b, c_2, norm_g_2, w_ada_2, b_ada_2, w_in_2,
    ln_v_g_2, ln_v_b_2, w_s_2, b_s_2, b_f_2, w_out_2, final_g_2,
):
    x = first_block(
        x, positions, emb_ln_g, emb_ln_b, w_in, q_norm_g, kv_norm_g, w_uq, w_ukv, w_pool,
        pool_scale, conv_w, w_out, b_out, ln_g, ln_b,
    )
    return second_block(
        x, c_2, norm_g_2, w_ada_2, b_ada_2, w_in_2, ln_v_g_2, ln_v_b_2, w_s_2, b_s_2, b_f_2,
        w_out_2, final_g_2,
    )


_drawn_inputs = setup_inputs


def setup_inputs(seed=0):
    import zlib

    import numpy as np

    out = dict(_drawn_inputs(seed))
    spreads = {}
    factors = {'emb_ln_g': 4.664,
     'emb_ln_b': 4.542,
     'q_norm_g': 8.0,
     'kv_norm_g': 8.0,
     'pool_scale': 3.975,
     'b_out': 39.936,
     'ln_g': 3.599,
     'ln_b': 3.256,
     'b_ada_2': 15.752,
     'ln_v_b_2': 64.0,
     'norm_g_2': 2.765,
     'ln_v_g_2': 6.971,
     'b_s_2': 6.475}
    for name, (base, spread) in spreads.items():
        noise = np.random.default_rng([zlib.crc32(name.encode()), seed]).standard_normal(out[name].shape)
        drawn = base * np.exp(spread * noise) if base else spread * noise
        out[name] = __import__('jax').numpy.asarray(drawn.astype(out[name].dtype))
    for name, factor in factors.items():
        out[name] = (out[name] * factor).astype(out[name].dtype)
    return out
```

```python
import numpy as np
import concourse.bass as bass
from concourse import mybir
from concourse.alu_op_type import AluOpType as ALU

F32, F32R, BF16, I32 = mybir.dt.float32, mybir.dt.float32r, mybir.dt.bfloat16, mybir.dt.int32
ACT = mybir.ActivationFunctionType
AXX = mybir.AxisListType.X

P = 128
NT = 512
D = 2048
KT = D // P
DEPTH = 2
HEADS, NOPE, ROPE, VDIM = 8, 128, 64, 128
Q_LORA, KV_LORA = 512, 256
QB = NT // P
UNIT = 1024
SLOTS = 4
GROUPS = 4
TAPS = 3
ALPHA = float((2 * DEPTH) ** 0.25)
LN_EPS, RMS_EPS = 1e-5, 1e-6
MLA_SCALE = float((NOPE + ROPE) ** -0.5)
MASKED = -1e30
TWO_PI = 2 * np.pi
PI_BELOW = float(np.nextafter(np.float32(np.pi), np.float32(0)))

T_GATE = 0
T_POOL = 8
T_CONV = 16
T_KV = 32
T_Q = 34
T_KR = 38
IN_TILES = 39
EV_TILES = 38
POS_HEAD = 2 * IN_TILES
POS_OUT = POS_HEAD + 2 * HEADS
LAYER_UNITS = POS_OUT + 2 * KT
MIX_ORDER = [0, 1, 2, 3, 4, 5, 6, 8, 9, 10, 11, 12, 13, 14, 15, 7]
HEAD_COLS = (512, 768)

B2_HEADS = 16
PAIRS = 8
DH2 = 64
A_HEADS = 8
WIDTH_A = 1024
B2 = DEPTH
Q2_SCALE = DH2 ** -0.5
T2_VA, T2_U, T2_GA, T2_F = 0, 8, 16, 24
T2_PAIR = 25
T2_OUT = T2_PAIR + 4 * PAIRS
B2_STEPS = T2_OUT + KT
B2_UNITS = 2 * B2_STEPS
HB = DEPTH * HEADS
ADA_TILES = 3 * KT
ADA_UNITS = 2 * ADA_TILES
ADA_LAYER = ADA_UNITS // DEPTH

C_QG, C_KVG, C_PS, C_CW, C_BO, C_LG, C_LB = 0, 4, 6, 10, 22, 38, 54
LAYER_COLS = 70
E_G, E_B, E_NG, E_FG, E_BADA, E_BF = 0, 16, 32, 48, 64, 112
EXTRA_COLS = 113

SB0 = 16512
KB = 1024
OFF_XH, OFF_XL, OFF_Y, OFF_G = 0, 32 * KB, 64 * KB, 96 * KB
OFF_RAW, OFF_WH, OFF_WL = 128 * KB, 144 * KB, 160 * KB
OFF_A = 176 * KB
OFF_TAB = 195 * KB
OFF_P = 197 * KB
OFF_T = 202 * KB
OFF_SM = 204 * KB
BYTES = 229344 - SB0


def poff(i):
    return P * i * (i + 1) // 2


def build(nc, layers, extra, stream, wada, wsT, wpool, rows, cond, positions, invf, xT, outT):
    from contextlib import ExitStack

    ctx = ExitStack()
    with ctx:
        used = set()

        def at(name, shape, dt, off):
            size = int(np.prod(shape[1:])) * (2 if dt == BF16 else 4)
            assert off + size <= BYTES, name
            assert name not in used
            used.add(name)
            return nc.alloc_sbuf_tensor_at(name, shape, dt, offset=SB0 + off)

        def sem(name):
            return ctx.enter_context(nc.semaphore(name))

        XH = at("x_hi", [P, KT, NT], F32R, OFF_XH)
        XL = at("x_lo", [P, KT, NT], F32R, OFF_XL)
        Y = at("x_res", [P, KT, NT], F32, OFF_Y)
        G = at("mix", [P, KT, NT], F32, OFF_G)
        RAW = at("w_raw", [P, SLOTS, UNIT], F32, OFF_RAW)
        WH = at("w_hi", [P, SLOTS, UNIT], F32R, OFF_WH)
        WL = at("w_lo", [P, SLOTS, UNIT], F32R, OFF_WL)
        QNH = at("qn_hi", [P, NT], F32R, OFF_A)
        QNL = at("qn_lo", [P, NT], F32R, OFF_A + 2 * KB)
        QR = at("q_rope", [P, NT], F32R, OFF_A + 4 * KB)
        PTH = [at("pt_hi0", [P, 3 * P], F32R, OFF_A + 6 * KB), at("pt_hi1", [P, NT], F32R, OFF_A + 9 * KB)]
        PTL = [at("pt_lo0", [P, 3 * P], F32R, OFF_A + 7 * KB + 512), at("pt_lo1", [P, NT], F32R, OFF_A + 11 * KB)]
        VSH = at("v_hi", [P, QB, VDIM], F32R, OFF_A + 13 * KB)
        VSL = at("v_lo", [P, QB, VDIM], F32R, OFF_A + 15 * KB)
        TV = at("v_t", [P, NT], F32, OFF_A + 17 * KB)
        PR = at("probs", [P, poff(QB)], F32, OFF_P)
        TR = at("rope_sum", [P, NT], F32, OFF_T)
        CS = at("cos_sin", [P, NT], F32, OFF_TAB)
        KH = at("k2_hi", [P, NT], F32R, OFF_A + 4 * KB)
        KL = at("k2_lo", [P, NT], F32R, OFF_T)
        F2 = at("log_gates", [P, NT], F32R, OFF_TAB)
        SQ2 = at("squares2", [P, KT, NT], F32, OFF_XH)
        H32 = at("h_unshifted", [P, KT, NT], F32, OFF_XL)
        VA = at("v_a", [P, QB, WIDTH_A], F32, OFF_A)
        BN = at("bn", [P, QB, 2, 6], F32, OFF_P)
        MV = at("mean_var", [P, QB, 2], F32, OFF_P + 256)
        WST = at("w_s", [P, A_HEADS, P], F32, OFF_G + 16 * KB)
        ROWS = at("row_params", [P, 3, WIDTH_A], F32, OFF_G + 20 * KB)
        CONDB = at("cond_b", [P, D], F32, OFF_A)
        ADAB = at("ada_w", [P, 2, UNIT], F32, OFF_A + 8 * KB)
        WP = at("w_pool", [P, GROUPS, P], F32, OFF_A + 16 * KB)
        LAT = at("latents", [P, 7, NT], F32, OFF_A)
        T0 = at("tmp0", [P, NT], F32, OFF_T)
        U = at("conv_u", [P, NT + TAPS - 1], F32, OFF_P)
        Y1 = at("tmp1", [P, NT], F32, OFF_P + 2 * KB + 512)
        SB = at("shift", [P, NT], F32, OFF_A)
        CT = at("centred", [P, NT], F32, OFF_A + 2 * KB)
        SQ = at("squares", [P, NT], F32, OFF_A + 4 * KB)
        A1 = at("sum1", [P, NT], F32, OFF_A + 6 * KB)
        A2 = at("sum2", [P, NT], F32, OFF_A + 8 * KB)
        DG = [at("diag0", [P, QB, P], F32, OFF_A + 10 * KB), at("diag1", [P, QB, P], F32, OFF_A + 12 * KB)]
        NBUF = (CT, SQ, A1, A2)
        small = {}
        o = OFF_SM
        for name, cols, dt in (("ident", P, F32), ("ones", P, F32), ("mask", P, BF16),
                               ("cols", DEPTH * LAYER_COLS, F32), ("ext_cols", EXTRA_COLS, F32),
                               ("mod_parts", ADA_UNITS, F32), ("stats", 32, F32), ("recips", 16, F32),
                               ("mod", ADA_TILES, F32), ("norm_gain", KT, F32), ("pick", 2 * B2_HEADS, F32R),
                               ("neg_pick1", P, F32R)):
            small[name] = at(name, [P, cols], dt, o)
            if name == "cols":
                assert DEPTH * LAYER_COLS >= P
                small["neg_pick0"] = at("neg_pick0", [P, P], F32R, o)
            o += -(-cols * (2 if dt == BF16 else 4) // 32) * 32
        IDN, ONES, MASK, COL, NP0, EXT, MODP, ST, RC, MOD, NG, PICK, NP1 = small.values()
        NPICK = (NP0, NP1)
        IDB = IDN[:, :].bitcast(BF16)[:, 1::2]

        PS = [ctx.enter_context(nc.psum_tensor(f"bank{i}", [P, NT], F32)) for i in range(8)]

        raw_in = [sem(f"raw_in{s}") for s in range(SLOTS)]
        w_hi, w_lo, w_used = sem("w_hi_s"), sem("w_lo_s"), sem("w_used")
        xt_in = [sem(f"xt_in{g}") for g in range(KT // 2)]
        names = ("const_in cols_in wpool_in cond_in ada_in0 ada_in1 pool_set ang rng dve_set cs_done "
                 "in_ev conv_ready pool_step pool_mm pool_ev conv_step conv_ev ada_done "
                 "sq_done sq_sum lat_mm lat_v lat_sd lat_ri lat_dg lat_bc lat_n lat_hi lat_lo "
                 "proj kn_hi kn_lo v_out v_tr v_hi v_lo qn_hi qn_lo rope_k rope_q qr_hi krh krl "
                 "s_mm s_max s_nb s_exp s_rc p_norm p_tr pt_hi pt_lo pv_mm pv_out "
                 "mix_hi mix_lo out_ev res "
                 "sh_mm sh_b zero ct c_sq sum1 sum2 st_mm st_v st_sd st_ri dg_m dg_r bc_m bc_r sh_tot "
                 "n_sub n_mul n_x x_lo_s stored "
                 "emb_sum emb_mm emb_v emb_sd h_hi cond_silu mod_set r_sq r_sum r_mm r_v r_sd r_ri r_dg r_bc h_mul rows_in ws_set "
                 "in2_ev ga_ev va_tr va_ev bn_set sg_sd sg_mul sg_v sg_mm sg_tmp sg_out "
                 "f_step f_act f2_hi f2_set npick out2_ev fin").split()
        S = {n: sem(n) for n in names}

        def col(l, c):
            return COL[:, bass.ds(l * LAYER_COLS + c, 1)]

        slot_uses = [len(range(s, LAYER_UNITS, SLOTS)) for s in range(SLOTS)]

        def unit(l, pos):
            return pos % SLOTS, l * LAYER_UNITS + pos, l * slot_uses[pos % SLOTS] + pos // SLOTS + 1

        def freed(l, pos):
            n = l * LAYER_UNITS + pos
            return n - 1 if pos < 2 else n - 3

        def step_done(l, s):
            return l * LAYER_UNITS + 2 * s + 2

        def step_units(l, s):
            if l < B2 and s >= LAYER_UNITS // 2:
                l, s = l + 1, s - LAYER_UNITS // 2
            cols = HEAD_COLS if l < B2 and IN_TILES <= s < IN_TILES + HEADS else (UNIT, UNIT)
            return l, 2 * s, cols

        def norm_uses(n, k):
            return 2 * KT * n + 2 * k + 2 if n < DEPTH else 2 * KT * n + k + 1

        def split_hi(act, l, s, units=(0, 1)):
            if l == B2 and s >= B2_STEPS:
                return
            l, pos, cols = step_units(l, s)
            for n in units:
                slot, before, uses = unit(l, pos + n)
                act.wait_ge(raw_in[slot], 16 * uses)
                if not (isinstance(l, int) and l == 0 and pos + n < SLOTS):
                    act.wait_ge(w_used, freed(l, pos + n))
                nc.scalar.activation(WH[:, slot, :cols[n]], RAW[:, slot, :cols[n]], ACT.Copy).then_inc(w_hi, 1)

        def split_lo(dve, l, s, units=(0, 1)):
            if l == B2 and s >= B2_STEPS:
                return
            l, pos, cols = step_units(l, s)
            for n in units:
                slot, before, uses = unit(l, pos + n)
                dve.wait_ge(w_hi, before + 1)
                nc.vector.tensor_tensor(out=WL[:, slot, :cols[n]], in0=RAW[:, slot, :cols[n]],
                                        in1=WH[:, slot, :cols[n]].bitcast(F32), op=ALU.subtract).then_inc(w_lo, 1)

        def products(out, wh, wl, xh, xl, first, last):
            nc.tensor.matmul(out, wh, xl, start=first, stop=False)
            nc.tensor.matmul(out, wl, xh, start=False, stop=False)
            return nc.tensor.matmul(out, wh, xh, start=False, stop=last)

        block = ctx.enter_context(nc.Block())

        @block.sync
        def _(sp):
            def load(l, pos):
                slot, before, uses = unit(l, pos)
                sp.dma_start(RAW[:, slot, :], stream[bass.ds(before, 1), :, :].rearrange("u p n -> p (u n)"))\
                  .then_inc(raw_in[slot], 16)

            sp.dma_start(CS[:, :].bitcast(I32), positions.broadcast_to([P, NT])).then_inc(S["const_in"], 16)
            sp.dma_start(ST[:, 0:3], invf).then_inc(S["const_in"], 16)
            for k in range(KT):
                sp.dma_start(Y[:, k, :], xT[k]).then_inc(xt_in[k // 2], 16)
                if k == 0:
                    sp.dma_start(EXT[:, :], extra).then_inc(S["cols_in"], 16)
                    sp.dma_start(COL[:, :], layers).then_inc(S["cols_in"], 16)
            for pos in range(SLOTS):
                load(0, pos)

            def layer(l):
                for pos in range(SLOTS, LAYER_UNITS + SLOTS):
                    ll, pp = (l, pos) if pos < LAYER_UNITS else (l + 1, pos - LAYER_UNITS)
                    sp.wait_ge(w_lo, freed(ll, pp))
                    load(ll, pp)

            for l in range(DEPTH):
                layer(l)
            for pos in range(SLOTS, B2_UNITS):
                sp.wait_ge(w_lo, freed(B2, pos))
                load(B2, pos)
            for m in range(KT):
                sp.wait_ge(S["fin"], m + 1)
                sp.dma_start(outT[m], Y[:, m, :]).then_inc(S["stored"], 16)
            sp.wait_ge(S["stored"], 16 * KT)

        @block.gpsimd
        def _(pool):
            nc.gpsimd.memset(IDN[:, :], 0.0).then_inc(S["pool_set"], 1)
            nc.gpsimd.memset(MASK[:, :], 0.0).then_inc(S["pool_set"], 1)
            nc.gpsimd.memset(ONES[:, :], 1.0).then_inc(S["pool_set"], 1)
            pool.wait_ge(S["pool_set"], 3)
            nc.gpsimd.affine_select(out=IDN[:, :], in_=IDN[:, :], compare_op=ALU.not_equal, fill=1.0, base=0,
                                    pattern=[[-1, P]], channel_multiplier=1).then_inc(S["pool_set"], 1)
            nc.gpsimd.affine_select(out=MASK[:, :], in_=MASK[:, :], compare_op=ALU.is_ge, fill=MASKED, base=0,
                                    pattern=[[-1, P]], channel_multiplier=1).then_inc(S["pool_set"], 1)

            def normalise_sub(n):
                pool.wait_ge(S["sh_tot"], n + 1)
                for k in range(KT):
                    buf = NBUF[k % 4]
                    if k >= 4:
                        pool.wait_ge(S["n_x"], norm_uses(n, k - 4))
                    nc.gpsimd.tensor_tensor(out=buf[:, :], in0=Y[:, k, :], in1=SB[:, :], op=ALU.subtract)\
                        .then_inc(S["n_sub"], 1)

            def softmax_norm(h8):
                for i in range(QB):
                    pool.wait_ge(S["s_rc"], QB * h8 + i + 1)
                    pi = PR[:, poff(i):poff(i + 1)]
                    nc.gpsimd.tensor_scalar(pi, pi, ST[:, 12 + i:13 + i], None, ALU.mult).then_inc(S["p_norm"], 1)

            def ada_load(l, n):
                if n >= 2:
                    pool.wait_ge(S["ada_done"], ADA_LAYER * l + n - 1)
                pool.dma_start(ADAB[:, n % 2, :], wada[bass.ds(ADA_LAYER * l + n, 1), :, :]
                               .rearrange("u p n -> p (u n)")).then_inc(S[f"ada_in{n % 2}"], 16)

            for k in range(1, KT):
                pool.wait_ge(S["ct"], k + 1)
                if k > 1:
                    pool.wait_ge(S["emb_sum"], k - 1)
                nc.gpsimd.tensor_tensor(out=A1[:, :], in0=Y[:, 0, :] if k == 1 else A1[:, :], in1=Y[:, k, :],
                                        op=ALU.add).then_inc(S["emb_sum"], 1)
            normalise_sub(0)

            def layer(l):
                pool.wait_ge(S["x_lo_s"], KT * (l + 1))
                pool.dma_start(WP[:, :, :], wpool[bass.ds(l, 1), :, :, :].rearrange("u p g n -> p (u g) n"))\
                    .then_inc(S["wpool_in"], 16)
                pool.dma_start(CONDB[:, :], cond.broadcast_to([P, D])).then_inc(S["cond_in"], 16)
                for n in range(2):
                    ada_load(l, n)
                for k in range(KT):
                    nc.gpsimd.tensor_scalar(Y[:, k, :], Y[:, k, :], ALPHA, col(l, C_BO + k), ALU.mult, ALU.add)\
                        .then_inc(S["res"], 1)
                for n in range(2, ADA_LAYER):
                    ada_load(l, n)
                for h in range(HEADS):
                    softmax_norm(HEADS * l + h)
                pool.wait_ge(S["pv_out"], HEADS * (l + 1))
                nc.gpsimd.memset(A1[:, :], 0.0).then_inc(S["zero"], 1)
                nc.gpsimd.memset(A2[:, :], 0.0).then_inc(S["zero"], 1)
                if l == DEPTH - 1:
                    pool.wait_ge(S["mix_lo"], KT * DEPTH)
                    pool.dma_start(WST[:, :, :], wsT).then_inc(S["rows_in"], 16)
                    pool.dma_start(ROWS[:, :, :], rows.broadcast_to([P, 3, WIDTH_A])).then_inc(S["rows_in"], 16)
                normalise_sub(l + 1)

            for l in range(DEPTH):
                layer(l)

            pool.wait_ge(S["rows_in"], 32)
            nc.gpsimd.affine_select(out=WST[:, :, :], in_=WST[:, :, :], compare_op=ALU.is_ge, fill=0.0, base=0,
                                    pattern=[[0, A_HEADS], [1, P]], channel_multiplier=-1).then_inc(S["ws_set"], 1)
            for t in range(QB):
                pool.wait_ge(S["bn_set"], 3 * QB + 2 + t + 1)
                nc.gpsimd.tensor_tensor(out=VA[:, t, :], in0=VA[:, t, :], in1=ROWS[:, 0, :], op=ALU.mult)\
                    .then_inc(S["sg_mul"], 1)
                pool.wait_ge(S["sg_mul"], t + 1)
                nc.gpsimd.tensor_tensor(out=VA[:, t, :], in0=VA[:, t, :], in1=ROWS[:, 1, :], op=ALU.add)\
                    .then_inc(S["sg_v"], 1)

            def neg_pick(h):
                if h >= 2:
                    pool.wait_ge(S["s_mm"], QB * (HB + h - 1))
                nc.gpsimd.tensor_scalar(NPICK[h % 2][:, :], ONES[:, :], -1.0,
                                        PICK[:, 2 * h:2 * h + 1].bitcast(F32), ALU.mult, ALU.mult).then_inc(S["npick"], 1)

            pool.wait_ge(S["f2_set"], 3)
            neg_pick(0)
            neg_pick(1)
            for h in range(B2_HEADS):
                softmax_norm(HB + h)
                if h + 2 < B2_HEADS:
                    neg_pick(h + 2)

        @block.scalar
        def _(act):
            def stat_square(n, k):
                act.wait_ge(S["ct"], KT * n + k + 1)
                act.wait_ge(S["sum2"], KT * (n - 1) + k)
                nc.scalar.activation(SQ[:, :], CT[:, :], ACT.Square).then_inc(S["c_sq"], 1)

            def stat_shift(n):
                act.wait_ge(S["sh_mm"], n + 1)
                nc.scalar.activation(SB[:, :], PS[2][:, :], ACT.Copy, scale=1.0 / P).then_inc(S["sh_b"], 1)

            def norm_end(n):
                if n:
                    act.wait_ge(S["st_v"], 4 * n)
                    nc.scalar.activation(ST[:, 24:28], ST[:, 20:24], ACT.Sqrt).then_inc(S["st_sd"], 1)
                if n == 0:
                    act.wait_ge(S["cols_in"], 32)
                for k in range(KT):
                    buf = NBUF[k % 4]
                    gain, offset = norm_cols(n, k)
                    act.wait_ge(S["n_mul"], KT * n + k + 1)
                    nc.scalar.activation(Y[:, k, :], buf[:, :], ACT.Identity, bias=offset, scale=gain)\
                        .then_inc(S["n_x"], 1)
                    if n == DEPTH:
                        act.wait_ge(S["n_x"], norm_uses(n, k))
                        nc.scalar.activation(SQ2[:, k, :], Y[:, k, :], ACT.Square).then_inc(S["r_sq"], 1)
                    else:
                        nc.scalar.activation(XH[:, k, :], buf[:, :], ACT.Identity, bias=offset, scale=gain)\
                            .then_inc(S["n_x"], 1)

            def norm_cols(n, k):
                if n == 0:
                    return EXT[:, E_G + k:E_G + k + 1], EXT[:, E_B + k:E_B + k + 1]
                return col(n - 1, C_LG + k), col(n - 1, C_LB + k)

            def split(l, s, units=(0, 1)):
                split_hi(act, l, s, units)

            act.wait_ge(S["ang"], 1)
            nc.scalar.activation(CS[:, :], T0[:, :], ACT.Sin).then_inc(S["cs_done"], 1)
            stat_shift(0)
            for k in range(KT):
                act.wait_ge(S["ct"], k + 1)
                nc.scalar.activation(SQ2[:, k, :], Y[:, k, :], ACT.Square).then_inc(S["c_sq"], 1)
            for s in range(2):
                split(0, s)
            act.wait_ge(S["emb_v"], 4)
            nc.scalar.activation(A2[:, :], A2[:, :], ACT.Sqrt).then_inc(S["emb_sd"], 1)
            norm_end(0)

            def layer(l):
                ev = lambda m: EV_TILES * l + m

                def evac(m, dst, func):
                    split(l, m + 2)
                    act.wait_ge(w_used, step_done(l, m))
                    return nc.scalar.activation(dst, PS[m % 2][:, :], func)

                for m in range(8):
                    evac(T_GATE + m, G[:, m, :], ACT.Silu).then_inc(S["in_ev"], 1)
                    if m == 0:
                        act.wait_ge(S["cond_in"], 16 * (l + 1))
                        nc.scalar.activation(CONDB[:, :], CONDB[:, :], ACT.Silu).then_inc(S["cond_silu"], 1)
                for j in range(GROUPS):
                    m = T_POOL + 2 * j
                    evac(m, G[:, 8 + j, :], ACT.Silu).then_inc(S["in_ev"], 1)
                    evac(m + 1, T0[:, :], ACT.Copy).then_inc(S["in_ev"], 1)
                for j in range(GROUPS):
                    m = T_CONV + 4 * j
                    act.wait_ge(S["conv_ev"], GROUPS * l + j)
                    if j == 0:
                        act.wait_ge(S["pool_step"], 32 * (l + 1))
                    evac(m, T0[:, :], ACT.Copy).then_inc(S["in_ev"], 1)
                    if j == 0:
                        act.wait_ge(S["pool_mm"], GROUPS * (l + 1))
                    evac(m + 1, Y1[:, :], ACT.Copy).then_inc(S["in_ev"], 1)
                    split(l, m + 4)
                    act.wait_ge(S["conv_step"], 5 * (GROUPS * l + j) + 1)
                    act.wait_ge(w_used, step_done(l, m + 2))
                    nc.scalar.activation(Y1[:, :], PS[m % 2][:, :], ACT.Copy).then_inc(S["in_ev"], 1)
                    evac(m + 3, G[:, 12 + j, :], ACT.Silu).then_inc(S["in_ev"], 1)
                act.wait_ge(S["conv_ev"], GROUPS * (l + 1))
                act.wait_ge(S["ada_done"], ADA_LAYER * (l + 1))
                for i in range(6):
                    m = T_KV + i
                    split(l, m + 2)
                    act.wait_ge(w_used, step_done(l, m))
                    nc.scalar.activation(LAT[:, i, :], PS[m % 2][:, :], ACT.Copy).then_inc(S["lat_hi"], 1)
                    if i == 2:
                        act.wait_ge(S["lat_bc"], 2 * l + 1)
                    if i >= 1:
                        act.wait_ge(S["sq_sum"], 4 * l + (0, 0, 1, 1, 2, 3)[i])
                    first = i in (0, 2)
                    nc.scalar.activation((T0 if first else Y1)[:, :], PS[m % 2][:, :], ACT.Square)\
                        .then_inc(S["in_ev"], 1)
                    if i == 1:
                        lat_sd(l, 0)
                split(l, T_KR + 2)
                lat_sd(l, 1)
                act.wait_ge(w_used, step_done(l, T_KR))
                for i in range(6):
                    act.wait_ge(S["lat_n"], 6 * l + i + 1)
                    nc.scalar.activation(XH[:, (12, 13, 8, 9, 10, 11)[i], :], LAT[:, i, :], ACT.Copy)\
                        .then_inc(S["krh"], 1)
                act.wait_ge(S["rope_k"], 4 * l + 4)
                nc.scalar.activation(XL[0:ROPE, 14, :], LAT[0:ROPE, 6, :], ACT.Copy).then_inc(S["krh"], 1)
                act.wait_ge(S["krh"], 8 * l + 7)
                nc.scalar.activation(XH[ROPE:P, 14, :], XL[0:ROPE, 14, :].bitcast(F32), ACT.Copy)\
                    .then_inc(S["krh"], 1)

                for h in range(HEADS):
                    hh = HEADS * l + h
                    act.wait_ge(S["proj"], 2 * hh + 1)
                    act.wait_ge(S["s_mm"], QB * hh)
                    nc.scalar.activation(XH[:, 15, :], PS[2][:, :], ACT.Copy).then_inc(S["kn_hi"], 1)
                    if h:
                        pt_hi(hh - 1, 0)
                    act.wait_ge(w_used, step_done(l, IN_TILES + h) - 1)
                    act.wait_ge(S["v_tr"], hh)
                    nc.scalar.activation(TV[:, :], PS[3][:, :], ACT.Copy).then_inc(S["v_out"], 1)
                    split(l, IN_TILES + h + 2, (0,))
                    if h:
                        pt_hi(hh - 1, 1)
                        pt_hi(hh - 1, 2)
                    act.wait_ge(w_used, step_done(l, IN_TILES + h))
                    nc.scalar.activation(QNH[:, :], PS[0][:, :], ACT.Copy).then_inc(S["qn_hi"], 1)
                    act.wait_ge(S["rope_q"], 5 * hh + 4)
                    nc.scalar.activation(QR[0:ROPE, :], TR[0:ROPE, :], ACT.Copy).then_inc(S["qr_hi"], 1)
                    if h:
                        pt_hi(hh - 1, 3)
                    split(l, IN_TILES + h + 2, (1,))
                    softmax_exp(hh, 0, MLA_SCALE)
                    act.wait_ge(S["v_tr"], hh + 1)
                    act.wait_ge(S["pv_mm"], QB * hh)
                    nc.scalar.activation(VSH[:, :, :], PS[3][:, :].rearrange("p (t d) -> p t d", t=QB), ACT.Copy)\
                        .then_inc(S["v_hi"], 1)
                    for i in range(1, QB):
                        softmax_exp(hh, i, MLA_SCALE)
                mix = [(k, n) for n, k in enumerate(MIX_ORDER)]
                for i in range(QB):
                    for k, n in mix[i:i + 1]:
                        to_mix(l, k, n)
                    pt_hi(HEADS * l + HEADS - 1, i)
                for k, n in mix[QB:]:
                    to_mix(l, k, n)
                for m in range(KT):
                    split(l, IN_TILES + HEADS + m + 2)
                    if m == 1:
                        stat_shift(l + 1)
                        stat_square(l + 1, 0)
                    if m >= 1:
                        stat_square(l + 1, m)
                norm_end(l + 1)

            def lat_sd(l, q):
                act.wait_ge(S["lat_v"], 2 * l + q + 1)
                nc.scalar.activation(ST[:, 24:28], ST[:, 20:24], ACT.Sqrt).then_inc(S["lat_sd"], 1)

            def pt_hi(hh, i):
                act.wait_ge(S["p_tr"], QB * hh + i + 1)
                act.wait_ge(S["pv_mm"], QB * hh + max(i - 1, 0))
                nc.scalar.activation(PTH[i % 2][:, :P * (i + 1)], PS[6 + i % 2][:, :P * (i + 1)], ACT.Copy)\
                    .then_inc(S["pt_hi"], 1)

            def softmax_exp(hh, i, scale):
                act.wait_ge(S["s_nb"], QB * hh + i + 1)
                act.wait_ge(S["p_tr"], QB * hh)
                nc.scalar.activation(PR[:, poff(i):poff(i + 1)], PS[5 - i % 2][:, :P * (i + 1)], ACT.Exp,
                                     bias=ST[:, 4 + i:5 + i], scale=scale,
                                     accum_out=ST[:, 8 + i:9 + i]).then_inc(S["s_exp"], 1)

            def to_mix(l, k, n):
                if k < 8:
                    act.wait_ge(S["pv_out"], HEADS * l + k + 1)
                act.wait_ge(S["s_mm"], QB * HEADS * (l + 1))
                nc.scalar.activation(XH[:, k, :], G[:, k, :], ACT.Copy).then_inc(S["mix_hi"], 1)

            for l in range(DEPTH):
                layer(l)

            def rms_sd(r):
                act.wait_ge(S["r_v"], r + 1)
                nc.scalar.activation(ST[:, 24:28], ST[:, 20:24], ACT.Sqrt).then_inc(S["r_sd"], 1)

            def half_split(s, n):
                split_hi(act, B2, s, (n,))

            act.wait_ge(S["r_v"], 1)
            nc.scalar.activation(A2[:, :], A2[:, :], ACT.Sqrt).then_inc(S["r_sd"], 1)
            for k in range(KT):
                act.wait_ge(S["h_mul"], k + 1)
                nc.scalar.activation(XH[:, k, :], H32[:, k, :], ACT.Identity, bias=MOD[:, k:k + 1])\
                    .then_inc(S["h_hi"], 1)
            for s in range(T2_F):
                j = s % 8
                split(B2, s + 2)
                act.wait_ge(w_used, step_done(B2, s))
                if s < T2_U:
                    if j >= 2:
                        act.wait_ge(S["va_tr"], j - 1)
                    nc.scalar.activation((T0, Y1)[j % 2][:, :], PS[s % 2][:, :], ACT.Gelu).then_inc(S["in2_ev"], 1)
                elif s < T2_GA:
                    nc.scalar.activation(G[:, j, :], PS[s % 2][:, :], ACT.Gelu).then_inc(S["in2_ev"], 1)
                else:
                    if j >= 2:
                        act.wait_ge(S["ga_ev"], j - 1)
                    nc.scalar.activation((T0, Y1)[j % 2][:, :], PS[s % 2][:, :], ACT.Silu).then_inc(S["in2_ev"], 1)
                if s == T2_U:
                    act.wait_ge(S["bn_set"], 3 * QB + 1)
                    nc.scalar.activation(ST[:, 24:28], ST[:, 20:24], ACT.Sqrt).then_inc(S["sg_sd"], 1)
            split(B2, T2_F + 2)
            act.wait_ge(S["f_step"], 3)
            nc.scalar.activation(Y1[0:16, :], Y1[0:16, :], ACT.Exp).then_inc(S["f_act"], 1)
            act.wait_ge(S["f_step"], 4)
            nc.scalar.activation(TV[0:16, :], U[0:16, 0:NT], ACT.Ln).then_inc(S["f_act"], 1)

            def q_hi(p):
                act.wait_ge(w_used, step_done(B2, T2_PAIR + 4 * p))
                act.wait_ge(S["s_mm"], QB * (HB + 2 * p))
                if p == 0:
                    act.wait_ge(S["sg_mm"], A_HEADS)
                nc.scalar.activation(QNH[:, :], PS[1][:, :], ACT.Copy, scale=Q2_SCALE).then_inc(S["qn_hi"], 1)

            for p in range(PAIRS):
                s, a = T2_PAIR + 4 * p, HB + 2 * p
                if p:
                    softmax_exp(a - 1, 3, 1.0)
                    pt_hi(a - 1, 0)
                    pt_hi(a - 1, 1)
                    pt_hi(a - 1, 2)
                    pt_hi(a - 1, 3)
                half_split(s + 2, 0)
                half_split(s + 2, 1)
                if p == 0:
                    act.wait_ge(S["f_step"], 11)
                    act.wait_ge(S["f2_set"], 1)
                    for r in (0, 64):
                        nc.scalar.activation(F2[r:r + 16, :], Y1[0:16, :], ACT.Copy).then_inc(S["f2_hi"], 1)
                    half_split(s + 3, 0)
                q_hi(p)
                if p:
                    half_split(s + 3, 0)
                half_split(s + 3, 1)
                act.wait_ge(w_used, step_done(B2, s + 1))
                nc.scalar.activation(KH[:, :], PS[0][:, :], ACT.Copy).then_inc(S["kn_hi"], 1)
                softmax_exp(a, 0, 1.0)
                softmax_exp(a, 1, 1.0)
                half_split(s + 4, 0)
                softmax_exp(a, 2, 1.0)
                softmax_exp(a, 3, 1.0)
                half_split(s + 4, 1)
                act.wait_ge(w_used, step_done(B2, s + 2))
                act.wait_ge(S["v_tr"], HB + p)
                nc.scalar.activation(TV[:, :], PS[1][:, :], ACT.Copy).then_inc(S["v_out"], 1)
                pt_hi(a, 0)
                act.wait_ge(S["v_tr"], HB + p + 1)
                act.wait_ge(S["pv_mm"], QB * a)
                nc.scalar.activation(VSH[:, :, :], PS[3][:, :].rearrange("p (t d) -> p t d", t=QB), ACT.Copy)\
                    .then_inc(S["v_hi"], 1)
                pt_hi(a, 1)
                pt_hi(a, 2)
                pt_hi(a, 3)
                half_split(s + 5, 0)
                softmax_exp(a + 1, 0, 1.0)
                softmax_exp(a + 1, 1, 1.0)
                half_split(s + 5, 1)
                softmax_exp(a + 1, 2, 1.0)
                act.wait_ge(w_used, step_done(B2, s + 3))
                if p == 0:
                    act.wait_ge(S["sg_out"], A_HEADS)
                nc.scalar.activation(G[:, 8 + p, :], PS[0][:, :], ACT.Silu).then_inc(S["in2_ev"], 1)
            last = HB + B2_HEADS - 1

            def mix2(k):
                if k >= 8:
                    act.wait_ge(S["pv_out"], HB + 2 * (k - 7))
                nc.scalar.activation(XH[:, k, :], G[:, k, :], ACT.Copy).then_inc(S["mix_hi"], 1)

            mix2(0)
            mix2(1)
            softmax_exp(last, 3, 1.0)
            k = 2
            for i in range(QB):
                mix2(k)
                mix2(k + 1)
                mix2(k + 2)
                k += 3
                pt_hi(last, i)
            mix2(14)
            half_split(T2_OUT + 2, 0)
            mix2(15)
            half_split(T2_OUT + 2, 1)
            for m in range(KT):
                if m:
                    split(B2, T2_OUT + m + 2)
                act.wait_ge(S["out2_ev"], m + 1)
                act.wait_ge(S["r_sum"], m)
                nc.scalar.activation(SQ[:, :], Y[:, m, :], ACT.Square).then_inc(S["r_sq"], 1)
            rms_sd(1)

        @block.vector
        def _(dve):
            V = nc.vector
            TT, TS, STT = V.tensor_tensor, V.tensor_scalar, V.scalar_tensor_tensor

            def split(l, s, units=(0, 1)):
                split_lo(dve, l, s, units)
                if l < B2 and 3 <= s <= T_KV + 1:
                    for n in range(ADA_LAYER * (s - 3) // (T_KV - 1), ADA_LAYER * (s - 2) // (T_KV - 1)):
                        ada(l, n)

            def ada(l, n):
                g = ADA_LAYER * l + n
                if n == 0:
                    dve.wait_ge(S["cond_silu"], l + 1)
                dve.wait_ge(S[f"ada_in{n % 2}"], 16 * (g // 2 + 1))
                STT(out=ADAB[:, n % 2, :], in0=ADAB[:, n % 2, :], scalar=1.0,
                    in1=CONDB[:, (n % 2) * UNIT:(n % 2 + 1) * UNIT], op0=ALU.mult, op1=ALU.mult,
                    accum_out=MODP[:, g:g + 1]).then_inc(S["ada_done"], 1)

            for t in range(16):
                V.memset(RC[:, t:t + 1], 1.0 / (t + 1))
            posf, turns = T0, Y1
            dve.wait_ge(S["const_in"], 32)
            n = 0

            def rot(ins):
                nonlocal n
                n += 1
                ins.then_inc(S["rng"], 1)
                dve.wait_ge(S["rng"], n)

            rot(V.tensor_copy(posf[:, :], CS[:, :].bitcast(I32)))
            rot(TS(posf[:, :], posf[:, :], ST[:, 0:1], None, ALU.mult))
            ROUND = 12582912.0
            rot(TS(turns[:, :], posf[:, :], 1.0 / TWO_PI, ST[:, 1:2], ALU.mult, ALU.add))
            rot(TS(turns[:, :], turns[:, :], ROUND, -ROUND, ALU.add, ALU.add))
            part1 = 6.28125
            part2 = float((np.float32(TWO_PI - part1).view(np.uint32) & np.uint32(0xFFFFF000)).view(np.float32))
            part3 = float(TWO_PI - part1 - part2)
            for part in (part1, part2, part3):
                rot(STT(out=posf[:, :], in0=turns[:, :], scalar=-part, in1=posf[:, :], op0=ALU.mult, op1=ALU.add))
            rot(TS(posf[:, :], posf[:, :], ST[:, 2:3], PI_BELOW, ALU.add, ALU.min))
            TS(posf[:, :], posf[:, :], -PI_BELOW, None, ALU.max).then_inc(S["ang"], 1)

            def stat(n, k):
                if k == 0:
                    dve.wait_ge(S["sh_b"], n + 1)
                dve.wait_ge(S["c_sq"], KT * n + k)
                dve.wait_ge(S["sum1"], KT * (n - 1) + k)
                TT(out=CT[:, :], in0=Y[:, k, :], in1=SB[:, :], op=ALU.subtract).then_inc(S["ct"], 1)
                dve.wait_ge(S["ct"], KT * n + k + 1)
                TT(out=A1[:, :], in0=A1[:, :], in1=CT[:, :], op=ALU.add).then_inc(S["sum1"], 1)
                dve.wait_ge(S["c_sq"], KT * n + k + 1)
                dve.wait_ge(S["sum2"], KT * (n - 1) + k)
                TT(out=A2[:, :], in0=A2[:, :], in1=SQ[:, :], op=ALU.add).then_inc(S["sum2"], 1)

            def rms_sum(k):
                dve.wait_ge(S["r_sq"], KT + k + 1)
                if k == 0:
                    V.tensor_copy(A1[:, :], SQ[:, :]).then_inc(S["r_sum"], 1)
                else:
                    dve.wait_ge(S["r_sum"], k)
                    TT(out=A1[:, :], in0=A1[:, :], in1=SQ[:, :], op=ALU.add).then_inc(S["r_sum"], 1)

            def rms_end():
                dve.wait_ge(S["r_mm"], 2)
                TS(ST[:, 20:24], PS[3][:, 0:4], 1.0 / D, RMS_EPS, ALU.mult, ALU.add).then_inc(S["r_v"], 1)
                dve.wait_ge(S["r_sd"], 2)
                V.reciprocal(ST[:, 28:32], ST[:, 24:28]).then_inc(S["r_ri"], 1)
                dve.wait_ge(S["r_ri"], 2)
                for t in range(QB):
                    TS(DG[1][:, t, :], IDN[:, :], ST[:, 28 + t:29 + t], None, ALU.mult).then_inc(S["r_dg"], 1)
                dve.wait_ge(S["r_bc"], 1)

            def emb_end():
                dve.wait_ge(S["emb_mm"], 1)
                TS(SB[:, :], PS[3][:, :], 1.0 / D, None, ALU.mult).then_inc(S["emb_v"], 1)
                dve.wait_ge(S["emb_v"], 1)
                TT(out=A1[:, :], in0=SB[:, :], in1=SB[:, :], op=ALU.mult).then_inc(S["emb_v"], 1)
                dve.wait_ge(S["emb_v"], 2)
                STT(out=A2[:, :], in0=PS[7][:, :], scalar=1.0 / D, in1=A1[:, :], op0=ALU.mult, op1=ALU.subtract)\
                    .then_inc(S["emb_v"], 1)
                dve.wait_ge(S["emb_v"], 3)
                TS(A2[:, :], A2[:, :], LN_EPS, None, ALU.add).then_inc(S["emb_v"], 1)
                dve.wait_ge(S["emb_sd"], 1)
                V.reciprocal(PS[7][:, :], A2[:, :]).then_inc(S["sh_tot"], 1)
                dve.wait_ge(S["sh_tot"], 1)

            def norm_end(n):
                dve.wait_ge(S["st_mm"], n)
                TS(ST[:, 16:24], PS[3][:, 0:8], 1.0 / D, None, ALU.mult).then_inc(S["st_v"], 1)
                dve.wait_ge(S["st_v"], 4 * n - 3)
                TT(out=ST[:, 28:32], in0=ST[:, 16:20], in1=ST[:, 16:20], op=ALU.mult).then_inc(S["st_v"], 1)
                dve.wait_ge(S["st_v"], 4 * n - 2)
                TT(out=ST[:, 20:24], in0=ST[:, 20:24], in1=ST[:, 28:32], op=ALU.subtract).then_inc(S["st_v"], 1)
                dve.wait_ge(S["st_v"], 4 * n - 1)
                TS(ST[:, 20:24], ST[:, 20:24], LN_EPS, None, ALU.add).then_inc(S["st_v"], 1)
                for t in range(QB):
                    TS(DG[0][:, t, :], IDN[:, :], ST[:, 16 + t:17 + t], None, ALU.mult).then_inc(S["dg_m"], 1)
                dve.wait_ge(S["st_sd"], n)
                V.reciprocal(ST[:, 28:32], ST[:, 24:28]).then_inc(S["st_ri"], 1)
                dve.wait_ge(S["st_ri"], n)
                for t in range(QB):
                    TS(DG[1][:, t, :], IDN[:, :], ST[:, 28 + t:29 + t], None, ALU.mult).then_inc(S["dg_r"], 1)
                dve.wait_ge(S["bc_m"], n)
                TT(out=SB[:, :], in0=SB[:, :], in1=PS[2][:, :], op=ALU.add).then_inc(S["sh_tot"], 1)
                dve.wait_ge(S["bc_r"], n)

            def normalise(n):
                def lo(k):
                    dve.wait_ge(S["n_x"], norm_uses(n, k))
                    TT(out=XL[:, k, :], in0=Y[:, k, :], in1=XH[:, k, :].bitcast(F32), op=ALU.subtract)\
                        .then_inc(S["x_lo_s"], 1)

                for k in range(KT):
                    buf = NBUF[k % 4]
                    dve.wait_ge(S["n_sub"], KT * n + k + 1)
                    TT(out=buf[:, :], in0=buf[:, :], in1=PS[7][:, :], op=ALU.mult).then_inc(S["n_mul"], 1)
                    if k >= 2 and n < DEPTH:
                        lo(k - 2)
                if n < DEPTH:
                    lo(KT - 2)
                    lo(KT - 1)

            dve.wait_ge(S["sh_b"], 1)
            for k in range(KT):
                dve.wait_ge(xt_in[k // 2], 32)
                TT(out=Y[:, k, :], in0=Y[:, k, :], in1=SB[:, :], op=ALU.subtract).then_inc(S["ct"], 1)
            for s in range(2):
                split(0, s)
            emb_end()
            normalise(0)

            def rope(src, cnt, base):
                TT(out=TR[0:ROPE, :], in0=src[0:ROPE, :], in1=CS[0:ROPE, :], op=ALU.mult).then_inc(cnt, 1)
                TT(out=src[64:96, :], in0=src[32:64, :], in1=CS[96:128, :], op=ALU.mult).then_inc(cnt, 1)
                TT(out=src[96:128, :], in0=src[0:32, :], in1=CS[64:96, :], op=ALU.mult).then_inc(cnt, 1)
                dve.wait_ge(cnt, base + 3)
                return TR[0:ROPE, :], src[64:128, :]

            def layer(l):
                iev = lambda m: EV_TILES * l + m + 1

                def pool_group(j):
                    w = 2 << j
                    step = 32 * l + (0, 5, 12, 21)[j]
                    src = T0
                    for d in range(j + 1):
                        dst, sh = (Y1, U)[d % 2], 1 << d
                        V.tensor_copy(dst[:, 0:sh], src[:, 0:sh]).then_inc(S["pool_step"], 1)
                        TT(out=dst[:, sh:NT], in0=src[:, sh:NT], in1=src[:, 0:NT - sh], op=ALU.add)\
                            .then_inc(S["pool_step"], 1)
                        step += 2
                        dve.wait_ge(S["pool_step"], step)
                        src = dst
                    z = (U, Y1)[j % 2]
                    STT(out=z[:, w - 1:NT], in0=src[:, w - 1:NT], scalar=1.0 / w, in1=T0[:, w - 1:NT],
                        op0=ALU.mult, op1=ALU.subtract).then_inc(S["pool_step"], 1)
                    TT(out=ST[:, 16:16 + w - 1], in0=src[:, 0:w - 1], in1=RC[:, 0:w - 1], op=ALU.mult)\
                        .then_inc(S["pool_step"], 1)
                    dve.wait_ge(S["pool_step"], step + 2)
                    TT(out=z[:, 0:w - 1], in0=ST[:, 16:16 + w - 1], in1=T0[:, 0:w - 1], op=ALU.subtract)\
                        .then_inc(S["pool_step"], 1)
                    dve.wait_ge(S["pool_step"], step + 3)

                def pool_out(j):
                    dve.wait_ge(S["pool_mm"], GROUPS * l + j + 1)
                    STT(out=G[:, 8 + j, :], in0=PS[4][:, :], scalar=col(l, C_PS + j), in1=G[:, 8 + j, :],
                        op0=ALU.mult, op1=ALU.mult).then_inc(S["pool_ev"], 1)

                for m in range(8):
                    split(l, m + 2)
                for j in range(GROUPS):
                    m = T_POOL + 2 * j
                    split(l, m + 2)
                    split(l, m + 3)
                    if j:
                        pool_out(j - 1)
                    dve.wait_ge(S["in_ev"], iev(m + 1))
                    pool_group(j)
                for j in range(GROUPS):
                    m = T_CONV + 4 * j
                    st = 5 * (GROUPS * l + j)
                    cw = lambda tap: col(l, C_CW + TAPS * j + tap)
                    split(l, m + 2)
                    split(l, m + 3)
                    if j == 0:
                        pool_out(GROUPS - 1)
                        V.memset(U[:, 0:TAPS - 1], 0.0).then_inc(S["conv_ready"], 1)
                        dve.wait_ge(S["conv_ready"], l + 1)
                    dve.wait_ge(S["in_ev"], iev(m + 1))
                    TT(out=U[:, 2:], in0=T0[:, :], in1=Y1[:, :], op=ALU.mult).then_inc(S["conv_step"], 1)
                    dve.wait_ge(S["conv_step"], st + 1)
                    TS(T0[:, :], U[:, 2:], cw(2), None, ALU.mult).then_inc(S["conv_step"], 1)
                    for tap in (1, 0):
                        dve.wait_ge(S["conv_step"], st + 3 - tap)
                        STT(out=T0[:, :], in0=U[:, tap:tap + NT], scalar=cw(tap), in1=T0[:, :],
                            op0=ALU.mult, op1=ALU.add).then_inc(S["conv_step"], 1)
                    split(l, m + 4)
                    dve.wait_ge(S["conv_step"], st + 4)
                    dve.wait_ge(S["in_ev"], iev(m + 2))
                    TT(out=T0[:, :], in0=T0[:, :], in1=Y1[:, :], op=ALU.mult).then_inc(S["conv_step"], 1)
                    split(l, m + 5)
                    dve.wait_ge(S["conv_step"], st + 5)
                    dve.wait_ge(S["in_ev"], iev(m + 3))
                    TT(out=G[:, 12 + j, :], in0=G[:, 12 + j, :], in1=T0[:, :], op=ALU.mult).then_inc(S["conv_ev"], 1)

                def lat_norm(q):
                    n = 2 * l + q
                    dve.wait_ge(S["lat_mm"], n + 1)
                    TS(ST[:, 20:24], PS[5][:, 0:4], 1.0 / (KV_LORA, Q_LORA)[q], RMS_EPS, ALU.mult, ALU.add)\
                        .then_inc(S["lat_v"], 1)
                    dve.wait_ge(S["lat_sd"], n + 1)
                    V.reciprocal(ST[:, 28:32], ST[:, 24:28]).then_inc(S["lat_ri"], 1)
                    dve.wait_ge(S["lat_ri"], n + 1)
                    for t in range(QB):
                        TS(T0[:, t * P:(t + 1) * P], IDN[:, :], ST[:, 28 + t:29 + t], None, ALU.mult)\
                            .then_inc(S["lat_dg"], 1)

                def lat_apply(q):
                    dve.wait_ge(S["lat_bc"], 2 * l + q + 1)
                    for i in ((0, 1), (2, 3, 4, 5))[q]:
                        g = col(l, C_KVG + i if q == 0 else C_QG + i - 2)
                        STT(out=LAT[:, i, :], in0=LAT[:, i, :], scalar=g, in1=PS[6][:, :], op0=ALU.mult,
                            op1=ALU.mult).then_inc(S["lat_n"], 1)

                if l == DEPTH - 1:
                    dve.wait_ge(S["ada_done"], ADA_UNITS)
                    TT(out=MOD[:, :], in0=MODP[:, 0::2], in1=MODP[:, 1::2], op=ALU.add).then_inc(S["mod_set"], 1)
                    dve.wait_ge(S["mod_set"], 1)
                    TT(out=MOD[:, :], in0=MOD[:, :], in1=EXT[:, E_BADA:E_BADA + ADA_TILES], op=ALU.add)\
                        .then_inc(S["mod_set"], 1)
                    dve.wait_ge(S["mod_set"], 2)
                    STT(out=NG[:, :], in0=MOD[:, KT:2 * KT], scalar=1.0, in1=EXT[:, E_NG:E_NG + KT],
                        op0=ALU.add, op1=ALU.mult).then_inc(S["mod_set"], 1)
                    dve.wait_ge(S["mod_set"], 3)
                sums = 0
                for i in range(6):
                    m = T_KV + i
                    split(l, m + 2)
                    if i not in (0, 2):
                        dve.wait_ge(S["in_ev"], iev(m))
                        dve.wait_ge(S["sq_sum"], 4 * l + sums)
                        TT(out=T0[:, :], in0=T0[:, :], in1=Y1[:, :], op=ALU.add).then_inc(S["sq_sum"], 1)
                        sums += 1
                    if i == 1:
                        lat_norm(0)
                    if i == 2:
                        lat_apply(0)
                split(l, T_KR + 2)
                lat_norm(1)
                lat_apply(1)
                dve.wait_ge(w_used, step_done(l, T_KR))
                dve.wait_ge(S["lat_dg"], 8 * (l + 1))
                a, b = rope(PS[7], S["rope_k"], 4 * l)
                TT(out=LAT[0:ROPE, 6, :], in0=a, in1=b, op=ALU.add).then_inc(S["rope_k"], 1)
                for i in range(6):
                    k = (12, 13, 8, 9, 10, 11)[i]
                    dve.wait_ge(S["krh"], 8 * l + i + 1)
                    TT(out=XL[:, k, :], in0=LAT[:, i, :], in1=XH[:, k, :].bitcast(F32), op=ALU.subtract)\
                        .then_inc(S["lat_lo"], 1)
                dve.wait_ge(S["krh"], 8 * l + 7)
                TT(out=XH[0:ROPE, 14, :], in0=LAT[0:ROPE, 6, :], in1=XL[0:ROPE, 14, :].bitcast(F32),
                   op=ALU.subtract).then_inc(S["krl"], 1)

                for h in range(HEADS):
                    hh = HEADS * l + h
                    dve.wait_ge(S["kn_hi"], hh + 1)
                    TT(out=XL[:, 15, :], in0=PS[2][:, :], in1=XH[:, 15, :].bitcast(F32), op=ALU.subtract)\
                        .then_inc(S["kn_lo"], 1)
                    if h:
                        pt_lo(hh - 1, 0)
                    split(l, IN_TILES + h + 2, (0,))
                    if h:
                        pt_lo(hh - 1, 1)
                    dve.wait_ge(S["proj"], 2 * hh + 2)
                    if h == 0:
                        dve.wait_ge(S["rope_k"], 4 * l + 4)
                    a, b = rope(PS[1], S["rope_q"], 5 * hh)
                    TT(out=a, in0=a, in1=b, op=ALU.add).then_inc(S["rope_q"], 1)
                    if h:
                        pt_lo(hh - 1, 2)
                    dve.wait_ge(S["qn_hi"], hh + 1)
                    TT(out=QNL[:, :], in0=PS[0][:, :], in1=QNH[:, :].bitcast(F32), op=ALU.subtract)\
                        .then_inc(S["qn_lo"], 1)
                    dve.wait_ge(S["qr_hi"], hh + 1)
                    TT(out=QR[ROPE:P, :], in0=TR[0:ROPE, :], in1=QR[0:ROPE, :].bitcast(F32), op=ALU.subtract)\
                        .then_inc(S["rope_q"], 1)
                    if h:
                        pt_lo(hh - 1, 3)
                    split(l, IN_TILES + h + 2, (1,))
                    row_max(hh, 0, MLA_SCALE)
                    if h:
                        head_out(hh - 1, h - 1)
                    dve.wait_ge(S["v_hi"], hh + 1)
                    TT(out=VSL[:, :, :], in0=PS[3][:, :].rearrange("p (t d) -> p t d", t=QB),
                       in1=VSH[:, :, :].bitcast(F32), op=ALU.subtract).then_inc(S["v_lo"], 1)
                    for i in range(1, QB):
                        row_max(hh, i, MLA_SCALE)
                        recip(hh, i - 1)
                    recip(hh, QB - 1)
                hh = HEADS * l + HEADS - 1
                for i in range(QB):
                    to_mix(l, i)
                    pt_lo(hh, i)
                for n in range(QB, QB + 2):
                    to_mix(l, n)
                head_out(hh, HEADS - 1)
                for n in range(QB + 2, KT):
                    to_mix(l, n)

                for m in range(KT):
                    split(l, IN_TILES + HEADS + m + 2)
                    dve.wait_ge(w_used, step_done(l, IN_TILES + HEADS + m))
                    if m == 0:
                        dve.wait_ge(S["res"], KT * (l + 1))
                    TT(out=Y[:, m, :], in0=Y[:, m, :], in1=PS[m % 2][:, :], op=ALU.add).then_inc(S["out_ev"], 1)
                    if m == 1:
                        dve.wait_ge(S["zero"], 2 * (l + 1))
                        stat(l + 1, 0)
                    if m >= 1:
                        dve.wait_ge(S["out_ev"], KT * l + m + 1)
                        stat(l + 1, m)
                norm_end(l + 1)
                normalise(l + 1)

            def pt_lo(hh, i):
                dve.wait_ge(S["pt_hi"], QB * hh + i + 1)
                TT(out=PTL[i % 2][:, :P * (i + 1)], in0=PS[6 + i % 2][:, :P * (i + 1)],
                   in1=PTH[i % 2][:, :P * (i + 1)].bitcast(F32), op=ALU.subtract).then_inc(S["pt_lo"], 1)

            def head_out(hh, h):
                dve.wait_ge(S["pv_mm"], QB * (hh + 1))
                TT(out=G[:, h, :], in0=PS[4][:, :], in1=G[:, h, :], op=ALU.mult).then_inc(S["pv_out"], 1)

            def recip(hh, i):
                dve.wait_ge(S["s_exp"], QB * hh + i + 1)
                V.reciprocal(ST[:, 12 + i:13 + i], ST[:, 8 + i:9 + i]).then_inc(S["s_rc"], 1)

            def row_max(hh, i, scale):
                dve.wait_ge(S["s_mm"], QB * hh + i + 1)
                if i == 0:
                    dve.wait_ge(S["p_norm"], QB * hh)
                V.reduce_max(ST[:, i:i + 1], PS[5 - i % 2][:, :P * (i + 1)], axis=AXX).then_inc(S["s_max"], 1)
                dve.wait_ge(S["s_max"], QB * hh + i + 1)
                TS(ST[:, 4 + i:5 + i], ST[:, i:i + 1], -scale, None, ALU.mult).then_inc(S["s_nb"], 1)

            def to_mix(l, n):
                k = MIX_ORDER[n]
                dve.wait_ge(S["mix_hi"], KT * l + n + 1)
                TT(out=XL[:, k, :], in0=G[:, k, :], in1=XH[:, k, :].bitcast(F32), op=ALU.subtract)\
                    .then_inc(S["mix_lo"], 1)

            for l in range(DEPTH):
                layer(l)

            def h_lo(k):
                dve.wait_ge(S["h_hi"], k + 1)
                STT(out=XL[:, k, :], in0=H32[:, k, :], scalar=MOD[:, k:k + 1], in1=XH[:, k, :].bitcast(F32),
                    op0=ALU.add, op1=ALU.subtract).then_inc(S["x_lo_s"], 1)

            dve.wait_ge(S["r_mm"], 1)
            TS(A2[:, :], PS[6][:, :], 1.0 / D, RMS_EPS, ALU.mult, ALU.add).then_inc(S["r_v"], 1)
            dve.wait_ge(S["r_sd"], 1)
            V.reciprocal(A2[:, :], A2[:, :]).then_inc(S["r_ri"], 1)
            dve.wait_ge(S["r_ri"], 1)
            for k in range(KT):
                STT(out=H32[:, k, :], in0=Y[:, k, :], scalar=NG[:, k:k + 1], in1=A2[:, :], op0=ALU.mult,
                    op1=ALU.mult).then_inc(S["h_mul"], 1)
                if k:
                    h_lo(k - 1)
            h_lo(KT - 1)

            def va_out(j):
                dve.wait_ge(S["va_tr"], j + 1)
                V.tensor_copy(VA[:, :, j * P:(j + 1) * P], PS[2 + j % 2][:, :].rearrange("p (t d) -> p t d", t=QB))\
                    .then_inc(S["va_ev"], 1)

            def va_norm():
                dve.wait_ge(S["va_ev"], A_HEADS)
                for t in range(QB):
                    for c in range(2):
                        V.bn_stats(BN[:, t, c, :], VA[:, t, c * NT:(c + 1) * NT]).then_inc(S["bn_set"], 1)
                dve.wait_ge(S["bn_set"], 2 * QB)
                for t in range(QB):
                    V.bn_aggr(MV[:, t, :], BN[:, t, :, :]).then_inc(S["bn_set"], 1)
                dve.wait_ge(S["bn_set"], 3 * QB)
                TS(ST[:, 20:24], MV[:, :, 1], RMS_EPS, None, ALU.add).then_inc(S["bn_set"], 1)
                split(B2, T2_U + 3)
                dve.wait_ge(S["sg_sd"], 1)
                V.reciprocal(ST[:, 28:32], ST[:, 24:28]).then_inc(S["bn_set"], 1)
                dve.wait_ge(S["bn_set"], 3 * QB + 2)
                for t in range(QB):
                    TS(VA[:, t, :], VA[:, t, :], MV[:, t, 0:1], ST[:, 28 + t:29 + t], ALU.subtract, ALU.mult)\
                        .then_inc(S["bn_set"], 1)

            for s in range(T2_F):
                if s != T2_U + 1:
                    split(B2, s + 2)
                j = s % 8
                if s == 2:
                    va_out(0)
                if 2 <= s <= T2_U:
                    va_out(s - 1)
                if s == T2_U:
                    va_norm()
                if s >= T2_GA:
                    dve.wait_ge(S["in2_ev"], s + 1)
                    TT(out=G[:, j, :], in0=G[:, j, :], in1=(T0, Y1)[j % 2][:, :], op=ALU.mult).then_inc(S["ga_ev"], 1)
            split(B2, T2_F + 2)
            fx, fe, fw, fl = T0[0:16, :], Y1[0:16, :], U[0:16, 0:NT], TV[0:16, :]
            dve.wait_ge(w_used, step_done(B2, T2_F))
            dve.wait_ge(S["ga_ev"], A_HEADS)
            TS(fx, PS[6][0:16, :], EXT[0:16, E_BF:E_BF + 1], None, ALU.add).then_inc(S["f_step"], 1)
            dve.wait_ge(S["f_step"], 1)
            TS(fe, fx, -1.0, None, ALU.mult).then_inc(S["f_step"], 1)
            dve.wait_ge(S["f_step"], 2)
            TT(out=fe, in0=fe, in1=fx, op=ALU.min).then_inc(S["f_step"], 1)
            dve.wait_ge(S["f_act"], 1)
            TS(fw, fe, 1.0, None, ALU.add).then_inc(S["f_step"], 1)
            TS(fx, fx, 0.0, None, ALU.min).then_inc(S["f_step"], 1)
            dve.wait_ge(S["f_step"], 4)
            STT(out=fe, in0=fw, scalar=-1.0, in1=fe, op0=ALU.add, op1=ALU.subtract).then_inc(S["f_step"], 1)
            dve.wait_ge(S["f_act"], 2)
            dve.wait_ge(S["f_step"], 6)
            V.reciprocal(fw, fw).then_inc(S["f_step"], 1)
            TT(out=fx, in0=fx, in1=fl, op=ALU.subtract).then_inc(S["f_step"], 1)
            dve.wait_ge(S["f_step"], 8)
            TT(out=fe, in0=fe, in1=fw, op=ALU.mult).then_inc(S["f_step"], 1)
            dve.wait_ge(S["f_step"], 9)
            TT(out=fx, in0=fx, in1=fe, op=ALU.add).then_inc(S["f_step"], 1)
            dve.wait_ge(S["f_step"], 10)
            V.tensor_tensor_scan(out=fe, data0=fx, data1=fx, initial=0.0, op0=ALU.add, op1=ALU.bypass)\
                .then_inc(S["f_step"], 1)
            TS(F2[:, :], CS[:, :], 0.0, None, ALU.mult).then_inc(S["f2_set"], 1)
            for r in (0, 64):
                twice = [IDN[r:r + DH2, c:c + B2_HEADS].rearrange("p (a b) -> p a b", b=1)
                         .broadcast_to([DH2, B2_HEADS, 2]) for c in (r, r + 32)]
                TT(out=PICK[r:r + DH2, :].rearrange("p (a b) -> p a b", b=2), in0=twice[0], in1=twice[1],
                   op=ALU.add).then_inc(S["f2_set"], 1)

            def half_split(s, n):
                split_lo(dve, B2, s, (n,))

            def gating(h):
                tmp = (T0[:, :], U[:, 0:NT])[h % 2]
                b_s = ROWS[:, 2:3, h * P:(h + 1) * P].broadcast_to([P, QB, P])
                dve.wait_ge(S["sg_mm"], h + 1)
                if h == 0:
                    dve.wait_ge(S["ga_ev"], A_HEADS)
                    dve.wait_ge(S["f_step"], 11)
                else:
                    dve.wait_ge(S["sg_out"], h)
                TT(out=tmp.rearrange("p (t d) -> p t d", t=QB), in0=PS[2 + h % 2][:, :]
                   .rearrange("p (t d) -> p t d", t=QB), in1=b_s, op=ALU.add).then_inc(S["sg_tmp"], 1)
                dve.wait_ge(S["sg_tmp"], h + 1)
                TT(out=G[:, h, :], in0=G[:, h, :], in1=tmp, op=ALU.mult).then_inc(S["sg_out"], 1)

            def pair_out(hh):
                p, r = (hh - HB) // 2, DH2 * (hh % 2)
                dve.wait_ge(S["in2_ev"], T2_F + p + 1)
                dve.wait_ge(S["pv_mm"], QB * (hh + 1))
                TT(out=G[r:r + DH2, 8 + p, :], in0=PS[2][0:DH2, :], in1=G[r:r + DH2, 8 + p, :], op=ALU.mult)\
                    .then_inc(S["pv_out"], 1)

            for p in range(PAIRS):
                s, a = T2_PAIR + 4 * p, HB + 2 * p
                if p:
                    pair_out(a - 2)
                    row_max(a - 1, 3, 1.0)
                    recip(a - 1, 2)
                    pt_lo(a - 1, 0)
                    recip(a - 1, 3)
                    pt_lo(a - 1, 1)
                    pt_lo(a - 1, 2)
                    pt_lo(a - 1, 3)
                half_split(s + 2, 0)
                if p:
                    pair_out(a - 1)
                half_split(s + 2, 1)
                if p == 0:
                    dve.wait_ge(S["f2_hi"], 2)
                    dve.wait_ge(S["f2_set"], 3)
                    for r in (32, 96):
                        TT(out=F2[r:r + 16, :], in0=fe, in1=F2[0:16, :].bitcast(F32), op=ALU.subtract)\
                            .then_inc(S["f2_set"], 1)
                    for h in range(4):
                        gating(h)
                    half_split(s + 3, 0)
                    for h in range(4, A_HEADS):
                        gating(h)
                dve.wait_ge(S["qn_hi"], HB + p + 1)
                STT(out=QNL[:, :], in0=PS[1][:, :], scalar=Q2_SCALE, in1=QNH[:, :].bitcast(F32), op0=ALU.mult,
                    op1=ALU.subtract).then_inc(S["qn_lo"], 1)
                if p:
                    half_split(s + 3, 0)
                half_split(s + 3, 1)
                dve.wait_ge(S["kn_hi"], HB + p + 1)
                TT(out=KL[:, :], in0=PS[0][:, :], in1=KH[:, :].bitcast(F32), op=ALU.subtract).then_inc(S["kn_lo"], 1)
                row_max(a, 0, 1.0)
                row_max(a, 1, 1.0)
                recip(a, 0)
                half_split(s + 4, 0)
                row_max(a, 2, 1.0)
                recip(a, 1)
                row_max(a, 3, 1.0)
                recip(a, 2)
                recip(a, 3)
                half_split(s + 4, 1)
                pt_lo(a, 0)
                dve.wait_ge(S["v_hi"], HB + p + 1)
                TT(out=VSL[:, :, :], in0=PS[3][:, :].rearrange("p (t d) -> p t d", t=QB),
                   in1=VSH[:, :, :].bitcast(F32), op=ALU.subtract).then_inc(S["v_lo"], 1)
                pt_lo(a, 1)
                pt_lo(a, 2)
                pt_lo(a, 3)
                half_split(s + 5, 0)
                row_max(a + 1, 0, 1.0)
                row_max(a + 1, 1, 1.0)
                recip(a + 1, 0)
                half_split(s + 5, 1)
                row_max(a + 1, 2, 1.0)
                recip(a + 1, 1)
            last = HB + B2_HEADS - 1

            def mix2_lo(k):
                dve.wait_ge(S["mix_hi"], KT * DEPTH + k + 1)
                TT(out=XL[:, k, :], in0=G[:, k, :], in1=XH[:, k, :].bitcast(F32), op=ALU.subtract)\
                    .then_inc(S["mix_lo"], 1)

            pair_out(last - 1)
            mix2_lo(0)
            mix2_lo(1)
            row_max(last, 3, 1.0)
            recip(last, 2)
            recip(last, 3)
            for i in range(QB):
                for k in range(2 + 3 * i, 5 + 3 * i):
                    mix2_lo(k)
                pt_lo(last, i)
            mix2_lo(14)
            half_split(T2_OUT + 2, 0)
            pair_out(last)
            mix2_lo(15)
            half_split(T2_OUT + 2, 1)
            for m in range(KT):
                if m:
                    split(B2, T2_OUT + m + 2)
                dve.wait_ge(w_used, step_done(B2, T2_OUT + m))
                STT(out=Y[:, m, :], in0=PS[(T2_OUT + m) % 2][:, :], scalar=MOD[:, 2 * KT + m:2 * KT + m + 1],
                    in1=Y[:, m, :], op0=ALU.mult, op1=ALU.add).then_inc(S["out2_ev"], 1)
                rms_sum(m)
            rms_end()
            for k in range(KT):
                STT(out=Y[:, k, :], in0=Y[:, k, :], scalar=EXT[:, E_FG + k:E_FG + k + 1], in1=PS[7][:, :],
                    op0=ALU.mult, op1=ALU.mult).then_inc(S["fin"], 1)

        @block.tensor
        def _(pe):
            mm = nc.tensor.matmul

            def column_sums(n):
                mm(PS[2][:, :], ONES[:, :], Y[:, 0, :], start=True, stop=True).then_inc(S["sh_mm"], 1)

            def norm_sums(n):
                pe.wait_ge(S["sum2"], KT * n)
                for a, acc in enumerate((A1, A2)):
                    for t in range(QB):
                        last = mm(PS[3][:, QB * a + t:QB * a + t + 1], acc[:, t * P:(t + 1) * P], ONES[:, 0:1],
                                  start=True, stop=True)
                last.then_inc(S["st_mm"], 1)
                for dg, s, bank, out in ((DG[0], S["dg_m"], 2, S["bc_m"]), (DG[1], S["dg_r"], 7, S["bc_r"])):
                    pe.wait_ge(s, QB * n)
                    for t in range(QB):
                        last = mm(PS[bank][:, t * P:(t + 1) * P], ONES[:, :], dg[:, t, :], start=True, stop=True)
                    last.then_inc(out, 1)

            pe.wait_ge(S["pool_set"], 5)
            pe.wait_ge(xt_in[0], 32)
            column_sums(0)
            for k in range(KT):
                pe.wait_ge(S["c_sq"], k + 1)
                mm(PS[7][:, :], ONES[:, :], SQ2[:, k, :], start=k == 0, stop=k == KT - 1)
            pe.wait_ge(S["emb_sum"], KT - 1)
            mm(PS[3][:, :], ONES[:, :], A1[:, :], start=True, stop=True).then_inc(S["emb_mm"], 1)

            def tile(l, s, bank, ready=None, order=range(KT), rows=P, mid={}):
                for n, k in enumerate(order):
                    half, col0 = n // 8, (n % 8) * P
                    slot, before, _ = unit(l, 2 * s + half)
                    if n % 8 == 0:
                        pe.wait_ge(w_lo, before + 1)
                    if ready:
                        pe.wait_ge(ready[0], ready[1] + n + 1)
                    last = products(PS[bank][:rows, :], WH[:, slot, col0:col0 + rows], WL[:, slot, col0:col0 + rows],
                                    XH[:, k, :], XL[:, k, :], n == 0, n == KT - 1)
                    if n % 8 == 7:
                        last.then_inc(w_used, 1)
                    for work in mid.get(n, ()):
                        work()
                return last

            def first_tiles(l):
                for k in range(KT):
                    half, col0 = k // 8, (k % 8) * P
                    if k % 8 == 0:
                        pe.wait_ge(w_lo, unit(l, 2 + half)[1] + 1)
                    pe.wait_ge(S["x_lo_s"], KT * l + k + 1)
                    for t in range(2):
                        slot = unit(l, 2 * t + half)[0]
                        last = products(PS[t][:, :], WH[:, slot, col0:col0 + P], WL[:, slot, col0:col0 + P],
                                        XH[:, k, :], XL[:, k, :], k == 0, k == KT - 1)
                        if k == KT - 1:
                            last.then_inc(w_used, 1 + t)
                    if k == 7:
                        last.then_inc(w_used, 1)

            def layer(l):

                def in_tile(m, mid={}):
                    if m < T_KR:
                        pe.wait_ge(S["in_ev"], EV_TILES * l + m - 1)
                    tile(l, m, m % 2 if m < T_KR else 7, rows=P if m < T_KR else ROPE, mid=mid)

                def pool_mm(j):
                    pe.wait_ge(S["pool_step"], 32 * l + (5, 12, 21, 32)[j])
                    pe.wait_ge(S["pool_ev"], GROUPS * l + j)
                    if j == 0:
                        pe.wait_ge(S["wpool_in"], 16 * (l + 1))
                    mm(PS[4][:, :], WP[:, j, :], ((U, Y1)[j % 2])[:, 0:NT], start=True, stop=True)\
                        .then_inc(S["pool_mm"], 1)

                def lat_sums(q):
                    n = 2 * l + q
                    pe.wait_ge(S["sq_sum"], 4 * l + (1, 4)[q])
                    for t in range(QB):
                        last = mm(PS[5][:, t:t + 1], T0[:, t * P:(t + 1) * P], ONES[:, 0:1], start=True, stop=True)
                    last.then_inc(S["lat_mm"], 1)

                def lat_bcast(q):
                    n = 2 * l + q
                    pe.wait_ge(S["lat_dg"], QB * (n + 1))
                    for t in range(QB):
                        last = mm(PS[6][:, t * P:(t + 1) * P], ONES[:, :], T0[:, t * P:(t + 1) * P],
                                  start=True, stop=True)
                    last.then_inc(S["lat_bc"], 1)

                first_tiles(l)
                for m in range(2, IN_TILES):
                    in_tile(m, {T_Q: {7: [lambda: lat_sums(0)]}, T_KR: {7: [lambda: lat_sums(1)]}}.get(m, {}))
                    if m in (10, 12, 14, 16):
                        pool_mm((m - 10) // 2)
                    if m == T_Q:
                        lat_bcast(0)
                lat_bcast(1)

                def head_proj(h):
                    hh = HEADS * l + h
                    slot, before, _ = unit(l, POS_HEAD + 2 * h)
                    pe.wait_ge(w_lo, before + 1)
                    if h == 0:
                        pe.wait_ge(S["lat_lo"], 6 * l + 2)
                    pv_ = lambda i: pv(hh - 1, i, PS[4], slice(0, VDIM), hh)
                    for n, (bank, c0, s, v) in enumerate(((2, 0, "kn_lo", hh), (3, 2 * P, "v_lo", hh))):
                        pe.wait_ge(S[s], v)
                        for k in range(2):
                            c = c0 + k * P
                            last = products(PS[bank][:, :], WH[:, slot, c:c + P], WL[:, slot, c:c + P],
                                            XH[:, 12 + k, :], XL[:, 12 + k, :], k == 0, k == 1)
                        if n == 0:
                            last.then_inc(S["proj"], 1)
                            if h:
                                trans(hh - 1, 0)
                    last.then_inc(w_used, 1)
                    if h:
                        trans(hh - 1, 1)
                    slot, before, _ = unit(l, POS_HEAD + 2 * h + 1)
                    pe.wait_ge(w_lo, before + 1)
                    if h == 0:
                        pe.wait_ge(S["lat_lo"], 6 * (l + 1))
                    pe.wait_ge(S["rope_q"], 5 * hh)
                    for k in range(4):
                        c = k * ROPE
                        last = products(PS[1][0:ROPE, :], WH[:, slot, c:c + ROPE], WL[:, slot, c:c + ROPE],
                                        XH[:, 8 + k, :], XL[:, 8 + k, :], k == 0, k == 3)
                    last.then_inc(S["proj"], 1)
                    if h:
                        pv_(0)
                        trans(hh - 1, 2)
                    pe.wait_ge(S["qn_lo"], hh)
                    for k in range(4):
                        c = 4 * ROPE + k * P
                        last = products(PS[0][:, :], WH[:, slot, c:c + P], WL[:, slot, c:c + P],
                                        XH[:, 8 + k, :], XL[:, 8 + k, :], k == 0, k == 3)
                    last.then_inc(w_used, 1)
                    if h:
                        pv_(1)
                        trans(hh - 1, 3)
                        pv_(2)
                        pv_(3)

                def v_transpose(hh):
                    pe.wait_ge(S["v_out"], hh + 1)
                    for t in range(QB):
                        last = nc.tensor.transpose(PS[3][:, t * P:(t + 1) * P], TV[:, t * P:(t + 1) * P], IDN[:, :])
                    last.then_inc(S["v_tr"], 1)

                def scores(hh, i):
                    bank, n = 5 - i % 2, P * (i + 1)
                    if i == 0:
                        for s, v in (("kn_lo", hh + 1), ("qn_lo", hh + 1), ("rope_q", 5 * hh + 5), ("krl", l + 1)):
                            pe.wait_ge(S[s], v)
                        pe.wait_ge(S["krh"], 8 * (l + 1))
                    pe.wait_ge(S["s_exp"], QB * hh + max(i - 1, 0))
                    if i == 1:
                        pe.wait_ge(S["pv_out"], hh)
                    q = slice(i * P, (i + 1) * P)
                    out = PS[bank][:, 0:n]
                    mm(out, QNH[:, q], XL[:, 15, 0:n], start=True, stop=False)
                    mm(out, QNL[:, q], XH[:, 15, 0:n], start=False, stop=False)
                    mm(out, QNH[:, q], XH[:, 15, 0:n], start=False, stop=False)
                    mm(out, QR[:, q], XH[:, 14, 0:n], start=False, stop=False)
                    mm(out, QR[0:ROPE, q], XL[0:ROPE, 14, 0:n], start=False, stop=False)
                    mm(PS[bank][:, n - P:n], IDB, MASK[:, :], start=False, stop=True).then_inc(S["s_mm"], 1)

                for h in range(HEADS):
                    head_proj(h)
                    for i in range(QB):
                        scores(HEADS * l + h, i)
                        if i == 0:
                            v_transpose(HEADS * l + h)
                attend(HEADS * l + HEADS - 1)
                for m in range(KT):
                    pe.wait_ge(S["out_ev"], KT * l + max(m - 1, 0))
                    tile(l, IN_TILES + HEADS + m, m % 2, (S["mix_lo"], KT * l) if m == 0 else None,
                         MIX_ORDER)
                    if m == 1:
                        pe.wait_ge(S["out_ev"], KT * l + 1)
                        column_sums(l + 1)
                norm_sums(l + 1)

            def trans(hh, i):
                pe.wait_ge(S["p_norm"], QB * hh + i + 1)
                pe.wait_ge(S["pt_lo"], QB * hh + max(i - 1, 0))
                for j in range(i + 1):
                    last = nc.tensor.transpose(PS[6 + i % 2][:, j * P:(j + 1) * P],
                                               PR[:, poff(i) + j * P:poff(i) + (j + 1) * P], IDN[:, :])
                last.then_inc(S["p_tr"], 1)

            def pv(hh, i, out, vcols, v_ready):
                pe.wait_ge(S["pt_lo"], QB * hh + i + 1)
                if i == 0:
                    pe.wait_ge(S["v_lo"], v_ready)
                    pe.wait_ge(S["pv_out"], hh)
                for j in range(i + 1):
                    c = slice(j * P, (j + 1) * P)
                    last = products(out[:, i * P:(i + 1) * P], VSH[:, j, vcols], VSL[:, j, vcols],
                                    PTH[i % 2][:, c], PTL[i % 2][:, c], j == 0, j == i)
                last.then_inc(S["pv_mm"], 1)

            def attend(hh):
                trans(hh, 0)
                for i in range(QB):
                    if i < QB - 1:
                        trans(hh, i + 1)
                    pv(hh, i, PS[4], slice(0, VDIM), hh + 1)

            for l in range(DEPTH):
                layer(l)

            def rms_sums():
                pe.wait_ge(S["r_sum"], KT)
                for t in range(QB):
                    last = mm(PS[3][:, t:t + 1], A1[:, t * P:(t + 1) * P], ONES[:, 0:1], start=True, stop=True)
                last.then_inc(S["r_mm"], 1)
                pe.wait_ge(S["r_dg"], QB)
                for t in range(QB):
                    last = mm(PS[7][:, t * P:(t + 1) * P], ONES[:, :], DG[1][:, t, :], start=True, stop=True)
                last.then_inc(S["r_bc"], 1)

            def va_trans(j):
                pe.wait_ge(S["in2_ev"], T2_VA + j + 1)
                pe.wait_ge(S["va_ev"], max(j - 1, 0))
                buf = (T0, Y1)[j % 2]
                for t in range(QB):
                    last = nc.tensor.transpose(PS[2 + j % 2][:, t * P:(t + 1) * P], buf[:, t * P:(t + 1) * P],
                                               IDN[:, :])
                last.then_inc(S["va_tr"], 1)

            def spatial(h):
                pe.wait_ge(S["sg_v"], QB)
                pe.wait_ge(S["ws_set"], 1)
                pe.wait_ge(S["sg_tmp"], max(h - 1, 0))
                for t in range(QB):
                    last = mm(PS[2 + h % 2][:, t * P:(t + 1) * P], VA[:, t, h * P:(h + 1) * P], WST[:, h, :],
                              start=True, stop=True)
                last.then_inc(S["sg_mm"], 1)

            def scores2(hh, i):
                bank, n, h = 5 - i % 2, P * (i + 1), hh - HB
                if i == 0:
                    pe.wait_ge(S["kn_lo"], HB + h // 2 + 1)
                    pe.wait_ge(S["qn_lo"], HB + h // 2 + 1)
                    pe.wait_ge(S["f2_set"], 5)
                    pe.wait_ge(S["npick"], h + 1)
                pe.wait_ge(S["s_exp"], QB * hh + max(i - 1, 0))
                q, r = slice(i * P, (i + 1) * P), slice(DH2 * (h % 2), DH2 * (h % 2 + 1))
                out = PS[bank][:, 0:n]
                mm(out, QNH[r, q], KL[r, 0:n], start=True, stop=False)
                mm(out, QNL[r, q], KH[r, 0:n], start=False, stop=False)
                mm(out, QNH[r, q], KH[r, 0:n], start=False, stop=False)
                mm(out, NPICK[h % 2][r, :], F2[r, 0:n], start=False, stop=False)
                pick = PICK[r, 2 * h:2 * h + 2].rearrange("p (a b) -> p a b", a=1).broadcast_to([DH2, n // 2, 2])
                mm(out, F2[r, q], pick, start=False, stop=False)
                mm(PS[bank][:, n - P:n], IDB, MASK[:, :], start=False, stop=True).then_inc(S["s_mm"], 1)

            def pv2(hh, i):
                h = hh - HB
                pv(hh, i, PS[2][0:DH2, :], slice(DH2 * (h % 2), DH2 * (h % 2 + 1)), HB + h // 2 + 1)

            def v_transpose2(p):
                pe.wait_ge(S["v_out"], HB + p + 1)
                pe.wait_ge(S["v_lo"], HB + p)
                for t in range(QB):
                    last = nc.tensor.transpose(PS[3][:, t * P:(t + 1) * P], TV[:, t * P:(t + 1) * P], IDN[:, :])
                last.then_inc(S["v_tr"], 1)

            for k in range(KT):
                pe.wait_ge(S["r_sq"], k + 1)
                last = mm(PS[6][:, :], ONES[:, :], SQ2[:, k, :], start=k == 0, stop=k == KT - 1)
            last.then_inc(S["r_mm"], 1)
            first_tiles(B2)
            for s in range(2, T2_F):
                pe.wait_ge(S["in2_ev"], s - 1)
                tile(B2, s, s % 2, mid={1: [lambda: va_trans(0)] if s == 2 else [],
                                        5: [lambda: va_trans(s - 1)] if s <= T2_U else []})
            tile(B2, T2_F, 6, rows=B2_HEADS)

            def do(f, *x):
                return lambda: f(*x)

            def second_half(hh):
                return {0: [do(scores2, hh, 3)], 2: [do(trans, hh, 0)], 4: [do(trans, hh, 1)],
                        6: [do(pv2, hh, 0), do(trans, hh, 2)], 8: [do(pv2, hh, 1), do(trans, hh, 3)],
                        10: [do(pv2, hh, 2)], 12: [do(pv2, hh, 3)]}

            for p in range(PAIRS):
                s, a = T2_PAIR + 4 * p, HB + 2 * p
                if p == 0:
                    pe.wait_ge(S["in2_ev"], T2_F)
                else:
                    pe.wait_ge(S["v_out"], HB + p)
                tile(B2, s, 1, mid=second_half(a - 1) if p else {})
                pe.wait_ge(S["in2_ev"], T2_F + p)
                tile(B2, s + 1, 0, mid={} if p else {2 * h: [do(spatial, h)] for h in range(A_HEADS)})
                pe.wait_ge(S["qn_lo"], HB + p + 1)
                tile(B2, s + 2, 1, mid={4 + 3 * i: [do(scores2, a, i)] for i in range(QB)})
                pe.wait_ge(S["kn_lo"], HB + p + 1)
                tile(B2, s + 3, 0, mid={
                    0: [do(trans, a, 0)], 2: [do(v_transpose2, p), do(trans, a, 1)],
                    5: [do(pv2, a, 0), do(trans, a, 2)], 7: [do(pv2, a, 1), do(trans, a, 3)],
                    9: [do(pv2, a, 2)], 11: [do(pv2, a, 3), do(scores2, a + 1, 0)],
                    13: [do(scores2, a + 1, 1)], 15: [do(scores2, a + 1, 2)]})
            for m in range(KT):
                if m == 0:
                    pe.wait_ge(S["v_out"], HB + PAIRS)
                elif m == 1:
                    pe.wait_ge(S["in2_ev"], T2_F + PAIRS)
                else:
                    pe.wait_ge(S["out2_ev"], m - 1)
                tile(B2, T2_OUT + m, (T2_OUT + m) % 2, (S["mix_lo"], KT * DEPTH) if m == 0 else None,
                     mid=second_half(HB + B2_HEADS - 1) if m == 0 else {})
            rms_sums()


IN_COLS = {"q": 0, "kv": 512, "kr": 768, "g_mla": 832, "p_in": 1856, "g_pool": 2368,
           "c_h": 2880, "c_b": 3392, "c_c": 3904, "g_conv": 4416}


def in_tiles():
    c = IN_COLS
    out = [c["g_mla"] + P * m for m in range(8)]
    for j in range(GROUPS):
        out += [c["g_pool"] + P * j, c["p_in"] + P * j]
    for j in range(GROUPS):
        out += [c[n] + P * j for n in ("c_h", "c_c", "c_b", "g_conv")]
    out += [c["kv"] + P * i for i in range(2)] + [c["q"] + P * i for i in range(4)] + [c["kr"]]
    return out


IN_COLS_2 = {"u": 0, "v": 1024, "g_a": 2048, "q": 3072, "k": 4096, "v_b": 5120, "g_b": 6144, "f": 7168}


def tile_units(w, c0, cols=P, order=None):
    t = np.zeros((P, KT, P), w.dtype)
    t[:, :, :cols] = w[:, c0:c0 + cols].reshape(KT, P, cols)[list(order or range(KT))].transpose(1, 0, 2)
    return [t[:, :8].reshape(P, UNIT), t[:, 8:].reshape(P, UNIT)]


def pack_stream(w_in, w_uq, w_ukv, w_out):
    units = []
    for l in range(DEPTH):
        for c0 in in_tiles():
            units += tile_units(w_in[l], c0, ROPE if c0 == IN_COLS["kr"] else P)
        uq = w_uq[l].reshape(4, P, HEADS, NOPE + ROPE)
        ukv = w_ukv[l].reshape(2, P, HEADS, NOPE + VDIM)
        for h in range(HEADS):
            kv, q = np.zeros((P, UNIT), w_in.dtype), np.zeros((P, UNIT), w_in.dtype)
            kv[:, :256] = ukv[:, :, h, :NOPE].transpose(1, 0, 2).reshape(P, 256)
            kv[:, 256:512] = ukv[:, :, h, NOPE:].transpose(1, 0, 2).reshape(P, 256)
            q[:, :256] = uq[:, :, h, NOPE:].transpose(1, 0, 2).reshape(P, 256)
            q[:, 256:768] = uq[:, :, h, :NOPE].transpose(1, 0, 2).reshape(P, 512)
            units += [kv, q]
        for m in range(KT):
            units += tile_units(w_out[l], P * m, order=MIX_ORDER)
    return units


def pack_stream_2(w_in, w_out):
    c = IN_COLS_2
    units = []
    for part in ("v", "u", "g_a"):
        for m in range(8):
            units += tile_units(w_in, c[part] + P * m)
    units += tile_units(w_in, c["f"], B2_HEADS)
    for p in range(PAIRS):
        for part in ("q", "k", "v_b", "g_b"):
            units += tile_units(w_in, c[part] + P * p)
    for m in range(KT):
        units += tile_units(w_out, P * m)
    return units


def columns(v):
    v = np.asarray(v)
    return v.reshape(-1, P).T


def kernel(**inputs):
    import concourse.bacc as bacc
    from concourse.bass_utils import run_bass_kernel_spmd

    a = {k: np.asarray(v) for k, v in inputs.items()}
    f32 = np.float32
    stream = np.stack(pack_stream(a["w_in"], a["w_uq"], a["w_ukv"], a["w_out"])
                      + pack_stream_2(a["w_in_2"][0], a["w_out_2"][0]))
    layers = np.concatenate([np.concatenate([
        columns(a["q_norm_g"][l]), columns(a["kv_norm_g"][l]), columns(a["pool_scale"][l]),
        a["conv_w"][l].reshape(TAPS, GROUPS, P).transpose(2, 1, 0).reshape(P, GROUPS * TAPS),
        columns(a["b_out"][l]), columns(a["ln_g"][l]), columns(a["ln_b"][l])], 1) for l in range(DEPTH)], 1)
    b_f = np.zeros((P, 1), f32)
    b_f[:B2_HEADS, 0] = a["b_f_2"][0]
    extra = np.concatenate([columns(a[n]) for n in ("emb_ln_g", "emb_ln_b", "norm_g_2", "final_g_2", "b_ada_2")]
                           + [b_f], 1)
    half = ROPE // 2
    freq = (10000.0 ** (-np.arange(half, dtype=f32) / half)).astype(f32)
    row = np.arange(P)
    phase = np.where(row < 64, np.pi / 2, np.where(row < 96, 0.0, np.pi))
    invf = np.stack([freq[row % half], phase / TWO_PI, phase], 1).astype(f32)
    arrays = {
        "layers": layers, "extra": extra, "stream": stream,
        "wada": a["w_ada_2"][0].T.reshape(ADA_TILES, P, 2, UNIT).transpose(0, 2, 1, 3)
        .reshape(ADA_UNITS, P, UNIT),
        "wsT": a["w_s_2"][0].transpose(2, 0, 1),
        "wpool": a["w_pool"].transpose(0, 2, 1, 3), "cond": a["c_2"].reshape(1, D),
        "rows": np.stack([a["ln_v_g_2"][0], a["ln_v_b_2"][0], a["b_s_2"][0].reshape(WIDTH_A)])[None],
        "positions": a["positions"].reshape(1, NT), "invf": invf,
        "xT": a["x"][0].T.reshape(KT, P, NT),
    }
    nc = bacc.Bacc("TRN2", target_bir_lowering=False, num_devices=1)
    aps = {}
    for name in list(arrays):
        arrays[name] = np.ascontiguousarray(arrays[name])
        aps[name] = nc.dram_tensor(name, arrays[name].shape, mybir.dt.from_np(arrays[name].dtype),
                                   kind="ExternalInput").ap()
    aps["outT"] = nc.dram_tensor("outT", (KT, P, NT), F32, kind="ExternalOutput").ap()
    build(nc, **aps)
    r = run_bass_kernel_spmd(nc, [arrays], core_ids=[0])
    return r.results[0]["outT"].reshape(D, NT).T[None]
```

```python
import numpy as np
import concourse.bass as bass
from concourse import mybir
from concourse.alu_op_type import AluOpType as ALU

F32, F32R, BF16, I32 = mybir.dt.float32, mybir.dt.float32r, mybir.dt.bfloat16, mybir.dt.int32
ACT = mybir.ActivationFunctionType
AXX = mybir.AxisListType.X

P = 128
NT = 512
D = 2048
KT = D // P
DEPTH = 2
HEADS, NOPE, ROPE, VDIM = 8, 128, 64, 128
Q_LORA, KV_LORA = 512, 256
QB = NT // P
UNIT = 1024
SLOTS = 4
GROUPS = 4
TAPS = 3
ALPHA = float((2 * DEPTH) ** 0.25)
LN_EPS, RMS_EPS = 1e-5, 1e-6
MLA_SCALE = float((NOPE + ROPE) ** -0.5)
MASKED = -1e30
TWO_PI = 2 * np.pi
PI_BELOW = float(np.nextafter(np.float32(np.pi), np.float32(0)))

T_KV = 0
T_Q = 2
T_KR = 6
T_POOL = 7
T_CONV = 15
T_GATE = 31
IN_TILES = 39
EV_TILES = 38
T_OUT = IN_TILES + HEADS
POS_HEAD = 2 * IN_TILES
POS_OUT = POS_HEAD + 2 * HEADS
LAYER_UNITS = POS_OUT + 2 * KT
MIX_ORDER = [0, 1, 2, 3, 4, 5, 6, 8, 9, 10, 11, 12, 13, 14, 15, 7]
LAT_TILES = ((8, 2), (9, 3), (10, 4), (11, 5), (12, 0), (13, 1))
HEAD_COLS = (512, 768)

B2_HEADS = 16
PAIRS = 8
DH2 = 64
A_HEADS = 8
WIDTH_A = 1024
B2 = DEPTH
Q2_SCALE = DH2 ** -0.5
T2_VA, T2_U, T2_GA, T2_F = 0, 8, 16, 24
T2_PAIR = 25
T2_OUT = T2_PAIR + 4 * PAIRS
B2_STEPS = T2_OUT + KT
B2_UNITS = 2 * B2_STEPS
MIX_BEHIND = ((3, 4), (5, 6, 7), (8, 9, 10), (11, 12, 13, 14))
HB = DEPTH * HEADS
ADA_TILES = 3 * KT
ADA_UNITS = 2 * ADA_TILES
ADA_LAYER = ADA_UNITS // DEPTH

C_QG, C_KVG, C_PS, C_CW, C_BO, C_LG, C_LB = 0, 4, 6, 10, 22, 38, 54
LAYER_COLS = 70
E_G, E_B, E_NG, E_FG, E_BADA, E_BF = 0, 16, 32, 48, 64, 112
EXTRA_COLS = 113

SB0 = 16512
KB = 1024
OFF_XH, OFF_XL, OFF_Y, OFF_G = 0, 32 * KB, 64 * KB, 96 * KB
OFF_RAW, OFF_WH, OFF_WL = 128 * KB, 144 * KB, 160 * KB
OFF_A = 176 * KB
OFF_TAB = 195 * KB
OFF_P = 197 * KB
OFF_T = 202 * KB
OFF_SM = 204 * KB
BYTES = 229344 - SB0


def poff(i):
    return P * i * (i + 1) // 2


def build(nc, layers, extra, stream, wada, wsT, wpool, rows, cond, positions, invf, xT, outT):
    from contextlib import ExitStack

    ctx = ExitStack()
    with ctx:
        used = set()

        def at(name, shape, dt, off):
            size = int(np.prod(shape[1:])) * (2 if dt == BF16 else 4)
            assert off + size <= BYTES, name
            assert name not in used
            used.add(name)
            return nc.alloc_sbuf_tensor_at(name, shape, dt, offset=SB0 + off)

        def sem(name):
            return ctx.enter_context(nc.semaphore(name))

        XH = at("x_hi", [P, KT, NT], F32R, OFF_XH)
        XL = at("x_lo", [P, KT, NT], F32R, OFF_XL)
        Y = at("x_res", [P, KT, NT], F32, OFF_Y)
        G = at("mix", [P, KT, NT], F32, OFF_G)
        RAW = at("w_raw", [P, SLOTS, UNIT], F32, OFF_RAW)
        WH = at("w_hi", [P, SLOTS, UNIT], F32R, OFF_WH)
        WL = at("w_lo", [P, SLOTS, UNIT], F32R, OFF_WL)
        QNH = at("qn_hi", [P, NT], F32R, OFF_A)
        QNL = at("qn_lo", [P, NT], F32R, OFF_A + 2 * KB)
        QR = at("q_rope", [P, NT], F32R, OFF_A + 4 * KB)
        PTH = [at("pt_hi0", [P, 3 * P], F32R, OFF_A + 6 * KB), at("pt_hi1", [P, NT], F32R, OFF_A + 9 * KB)]
        PTL = [at("pt_lo0", [P, 3 * P], F32R, OFF_A + 7 * KB + 512), at("pt_lo1", [P, NT], F32R, OFF_A + 11 * KB)]
        VSH = at("v_hi", [P, QB, VDIM], F32R, OFF_A + 13 * KB)
        VSL = at("v_lo", [P, QB, VDIM], F32R, OFF_A + 15 * KB)
        TV = at("v_t", [P, NT], F32, OFF_A + 17 * KB)
        PR = at("probs", [P, poff(QB)], F32, OFF_P)
        TR = at("rope_sum", [P, NT], F32, OFF_T)
        CS = at("cos_sin", [P, NT], F32, OFF_TAB)
        KH = at("k2_hi", [P, NT], F32R, OFF_A + 4 * KB)
        KL = at("k2_lo", [P, NT], F32R, OFF_T)
        F2 = at("log_gates", [P, NT], F32R, OFF_TAB)
        SQ2 = at("squares2", [P, KT, NT], F32, OFF_XH)
        H32 = at("h_unshifted", [P, KT, NT], F32, OFF_XL)
        VA = at("v_a", [P, QB, WIDTH_A], F32, OFF_A)
        BN = at("bn", [P, QB, 2, 6], F32, OFF_P)
        MV = at("mean_var", [P, QB, 2], F32, OFF_P + 256)
        WST = at("w_s", [P, A_HEADS, P], F32, OFF_G + 16 * KB)
        ROWS = at("row_params", [P, 3, WIDTH_A], F32, OFF_G + 20 * KB)
        CONDB = at("cond_b", [P, D], F32, OFF_G)
        ADAB = at("ada_w", [P, 2, UNIT], F32, OFF_G + 8 * KB)
        WP = at("w_pool", [P, GROUPS, P], F32, OFF_A + 16 * KB)
        LAT = at("latents", [P, 7, NT], F32, OFF_A)
        T0 = at("tmp0", [P, NT], F32, OFF_T)
        U = at("conv_u", [P, NT + TAPS - 1], F32, OFF_P)
        Y1 = at("tmp1", [P, NT], F32, OFF_P + 2 * KB + 512)
        SB = at("shift", [P, NT], F32, OFF_A)
        CT = at("centred", [P, NT], F32, OFF_A + 2 * KB)
        SQ = at("squares", [P, NT], F32, OFF_A + 4 * KB)
        A1 = at("sum1", [P, NT], F32, OFF_A + 6 * KB)
        A2 = at("sum2", [P, NT], F32, OFF_A + 8 * KB)
        DG = [at("diag0", [P, QB, P], F32, OFF_A + 10 * KB), at("diag1", [P, QB, P], F32, OFF_A + 12 * KB)]
        NBUF = (CT, SQ, A1, A2)
        small = {}
        o = OFF_SM
        for name, cols, dt in (("ident", P, F32), ("ones", P, F32), ("mask", P, BF16),
                               ("cols", DEPTH * LAYER_COLS, F32), ("ext_cols", EXTRA_COLS, F32),
                               ("mod_parts", ADA_UNITS, F32), ("stats", 32, F32), ("recips", 16, F32),
                               ("mod", ADA_TILES, F32), ("norm_gain", KT, F32), ("picks", B2_HEADS, F32),
                               ("neg_pick1", P, F32R), ("pick0", 2, F32R), ("pick1", 2, F32R)):
            small[name] = at(name, [P, cols], dt, o)
            if name == "cols":
                assert DEPTH * LAYER_COLS >= P
                small["neg_pick0"] = at("neg_pick0", [P, P], F32R, o)
            o += -(-cols * (2 if dt == BF16 else 4) // 32) * 32
        IDN, ONES, MASK, COL, NP0, EXT, MODP, ST, RC, MOD, NG, PICK, NP1, PP0, PP1 = small.values()
        NPICK, PPICK = (NP0, NP1), (PP0, PP1)
        IDB = IDN[:, :].bitcast(BF16)[:, 1::2]

        PS = [ctx.enter_context(nc.psum_tensor(f"bank{i}", [P, NT], F32)) for i in range(8)]

        raw_in = [sem(f"raw_in{s}") for s in range(SLOTS)]
        w_hi, w_lo, w_used = sem("w_hi_s"), sem("w_lo_s"), sem("w_used")
        xt_in = [sem(f"xt_in{g}") for g in range(KT // 2)]
        names = ("const_in cols_in wpool_in cond_in ada_in0 ada_in1 pool_set ang rng dve_set cs_done "
                 "in_ev conv_ready pool_step pool_mm pool_ev conv_step conv_ev ada_done "
                 "sq_done sq_sum lat_mm lat_v lat_sd lat_ri lat_dg lat_bc lat_n lat_hi lat_lo "
                 "proj kn_hi kn_lo v_out v_tr v_hi v_lo qn_hi qn_lo rope_k rope_q qr_hi krh krl "
                 "s_mm s_max s_nb s_exp s_rc p_norm p_tr pt_hi pt_lo pv_mm pv_out "
                 "mix_hi mix_lo out_ev res "
                 "sh_mm sh_b zero ct c_sq sum1 sum2 st_mm st_v st_sd st_ri dg_m dg_r bc_m bc_r sh_tot "
                 "n_sub n_mul n_x x_lo_s stored "
                 "emb_sum emb_mm emb_v emb_sd h_hi cond_silu mod_set r_sq r_sum r_mm r_v r_sd r_ri r_dg r_bc h_mul rows_in ws_set "
                 "in2_ev ga_ev va_tr va_ev bn_set sg_sd sg_mul sg_v sg_mm sg_tmp sg_out "
                 "f_step f_act f2_hi f2_set npick out2_ev fin").split()
        S = {n: sem(n) for n in names}

        def col(l, c):
            return COL[:, bass.ds(l * LAYER_COLS + c, 1)]

        slot_uses = [len(range(s, LAYER_UNITS, SLOTS)) for s in range(SLOTS)]

        def unit(l, pos, i=0):
            return (pos % SLOTS, l * LAYER_UNITS + pos + SLOTS * i,
                    l * slot_uses[pos % SLOTS] + pos // SLOTS + 1 + i)

        def freed(l, pos, i=0):
            return l * LAYER_UNITS + pos + SLOTS * i - (1 if pos < 2 else 3)

        def step_done(l, s, i=0):
            return l * LAYER_UNITS + 2 * s + 2 + SLOTS * i

        def step_units(l, s):
            if l < B2 and s >= LAYER_UNITS // 2:
                l, s = l + 1, s - LAYER_UNITS // 2
            cols = HEAD_COLS if l < B2 and IN_TILES <= s < IN_TILES + HEADS else (UNIT, UNIT)
            return l, 2 * s, cols

        def feature(t, k):
            return t[:, k, :] if isinstance(k, int) else t[:, bass.ds(k, 1), :].rearrange("p k n -> p (k n)")

        def column(t, c):
            return t[:, c:c + 1] if isinstance(c, int) else t[:, bass.ds(c, 1)]

        def taken(l, m):
            return EV_TILES * l + m + 1 - (m >= T_KR)

        def norm_uses(n, k):
            return 2 * KT * n + 2 * k + 2 if n < DEPTH else 2 * KT * n + k + 1

        def split_hi(act, l, s, units=(0, 1), i=0):
            if l == B2 and s >= B2_STEPS:
                return
            l, pos, cols = step_units(l, s)
            for n in units:
                slot, before, uses = unit(l, pos + n, i)
                act.wait_ge(raw_in[slot], 16 * uses)
                if not (isinstance(l, int) and l == 0 and pos + n < SLOTS):
                    act.wait_ge(w_used, freed(l, pos + n, i))
                nc.scalar.activation(WH[:, slot, :cols[n]], RAW[:, slot, :cols[n]], ACT.Copy).then_inc(w_hi, 1)

        def split_lo(dve, l, s, units=(0, 1), i=0):
            if l == B2 and s >= B2_STEPS:
                return
            l, pos, cols = step_units(l, s)
            for n in units:
                slot, before, uses = unit(l, pos + n, i)
                dve.wait_ge(w_hi, before + 1)
                nc.vector.tensor_tensor(out=WL[:, slot, :cols[n]], in0=RAW[:, slot, :cols[n]],
                                        in1=WH[:, slot, :cols[n]].bitcast(F32), op=ALU.subtract).then_inc(w_lo, 1)

        def products(out, wh, wl, xh, xl, first, last):
            nc.tensor.matmul(out, wh, xl, start=first, stop=False)
            nc.tensor.matmul(out, wl, xh, start=False, stop=False)
            return nc.tensor.matmul(out, wh, xh, start=False, stop=last)

        block = ctx.enter_context(nc.Block())

        @block.sync
        def _(sp):
            def load(l, pos, i=0):
                slot, before, uses = unit(l, pos, i)
                if not (isinstance(l, int) and l == 0 and pos < SLOTS):
                    sp.wait_ge(w_lo, freed(l, pos, i))
                sp.dma_start(RAW[:, slot, :], stream[bass.ds(before, 1), :, :].rearrange("u p n -> p (u n)"))\
                  .then_inc(raw_in[slot], 16)

            sp.dma_start(CS[:, :].bitcast(I32), positions.broadcast_to([P, NT])).then_inc(S["const_in"], 16)
            sp.dma_start(ST[:, 0:3], invf).then_inc(S["const_in"], 16)
            for k in range(KT):
                sp.dma_start(Y[:, k, :], xT[k]).then_inc(xt_in[k // 2], 16)
                if k == 0:
                    sp.dma_start(EXT[:, :], extra).then_inc(S["cols_in"], 16)
                    sp.dma_start(COL[:, :], layers).then_inc(S["cols_in"], 16)
            for pos in range(SLOTS):
                load(0, pos)

            for l, units in ((0, LAYER_UNITS), (1, LAYER_UNITS), (B2, B2_UNITS)):
                rounds = units // SLOTS
                with sp.Fori(0, rounds - 1) as i:
                    for pos in range(SLOTS, 2 * SLOTS):
                        load(l, pos, i)
                for pos in range(SLOTS * rounds, units):
                    load(l, pos)
                if l < B2:
                    for pos in range(SLOTS):
                        load(l + 1, pos)
            for m in range(KT):
                sp.wait_ge(S["fin"], m + 1)
                sp.dma_start(outT[m], Y[:, m, :]).then_inc(S["stored"], 16)
            sp.wait_ge(S["stored"], 16 * KT)

        @block.gpsimd
        def _(pool):
            nc.gpsimd.memset(IDN[:, :], 0.0).then_inc(S["pool_set"], 1)
            nc.gpsimd.memset(MASK[:, :], 0.0).then_inc(S["pool_set"], 1)
            nc.gpsimd.memset(ONES[:, :], 1.0).then_inc(S["pool_set"], 1)
            pool.wait_ge(S["pool_set"], 3)
            nc.gpsimd.affine_select(out=IDN[:, :], in_=IDN[:, :], compare_op=ALU.not_equal, fill=1.0, base=0,
                                    pattern=[[-1, P]], channel_multiplier=1).then_inc(S["pool_set"], 1)
            nc.gpsimd.affine_select(out=MASK[:, :], in_=MASK[:, :], compare_op=ALU.is_ge, fill=MASKED, base=0,
                                    pattern=[[-1, P]], channel_multiplier=1).then_inc(S["pool_set"], 1)

            def normalise_sub(n):
                pool.wait_ge(S["sh_tot"], n + 1)
                def sub(k, i=None):
                    if i is not None:
                        pool.wait_ge(S["n_x"], norm_uses(n, k) + i * (8 if n < DEPTH else 4))
                        k = 4 * (i + 1) + k
                    nc.gpsimd.tensor_tensor(out=NBUF[b][:, :], in0=feature(Y, k), in1=SB[:, :], op=ALU.subtract)\
                        .then_inc(S["n_sub"], 1)

                for b in range(4):
                    sub(b)
                with pool.Fori(0, KT // 4 - 1) as i:
                    for b in range(4):
                        sub(b, i)

            def softmax_norm(h8):
                for i in range(QB):
                    pool.wait_ge(S["s_rc"], QB * h8 + i + 1)
                    pi = PR[:, poff(i):poff(i + 1)]
                    nc.gpsimd.tensor_scalar(pi, pi, ST[:, 12 + i:13 + i], None, ALU.mult).then_inc(S["p_norm"], 1)

            def ada_load(l, n, i=0):
                if not isinstance(i, int):
                    pool.wait_ge(S["ada_done"], ADA_LAYER * l + n - 1 + 2 * i)
                pool.dma_start(ADAB[:, n, :], wada[bass.ds(ADA_LAYER * l + n + 2 * i, 1), :, :]
                               .rearrange("u p n -> p (u n)")).then_inc(S[f"ada_in{n}"], 16)

            for k in range(1, KT):
                pool.wait_ge(S["ct"], k + 1)
                if k > 1:
                    pool.wait_ge(S["emb_sum"], k - 1)
                nc.gpsimd.tensor_tensor(out=A1[:, :], in0=Y[:, 0, :] if k == 1 else A1[:, :], in1=Y[:, k, :],
                                        op=ALU.add).then_inc(S["emb_sum"], 1)
            normalise_sub(0)

            def layer(l):
                pool.wait_ge(S["x_lo_s"], KT * (l + 1))
                pool.dma_start(WP[:, :, :], wpool[bass.ds(l, 1), :, :, :].rearrange("u p g n -> p (u g) n"))\
                    .then_inc(S["wpool_in"], 16)
                pool.dma_start(CONDB[:, :], cond.broadcast_to([P, D])).then_inc(S["cond_in"], 16)
                for n in range(2):
                    ada_load(l, n)
                for k in range(KT):
                    nc.gpsimd.tensor_scalar(feature(Y, k), feature(Y, k), ALPHA, col(l, C_BO + k), ALU.mult, ALU.add)\
                        .then_inc(S["res"], 1)
                with pool.Fori(1, ADA_LAYER // 2) as i:
                    for n in range(2):
                        ada_load(l, n, i)
                for h in range(HEADS):
                    softmax_norm(HEADS * l + h)
                pool.wait_ge(S["pv_out"], HEADS * (l + 1))
                nc.gpsimd.memset(A1[:, :], 0.0).then_inc(S["zero"], 1)
                nc.gpsimd.memset(A2[:, :], 0.0).then_inc(S["zero"], 1)
                if l == DEPTH - 1:
                    pool.wait_ge(S["mix_lo"], KT * DEPTH)
                    pool.dma_start(WST[:, :, :], wsT).then_inc(S["rows_in"], 16)
                    pool.dma_start(ROWS[:, :, :], rows.broadcast_to([P, 3, WIDTH_A])).then_inc(S["rows_in"], 16)
                normalise_sub(l + 1)

            for l in range(DEPTH):
                layer(l)

            pool.wait_ge(S["rows_in"], 32)
            nc.gpsimd.affine_select(out=WST[:, :, :], in_=WST[:, :, :], compare_op=ALU.is_ge, fill=0.0, base=0,
                                    pattern=[[0, A_HEADS], [1, P]], channel_multiplier=-1).then_inc(S["ws_set"], 1)
            for t in range(QB):
                pool.wait_ge(S["bn_set"], 3 * QB + 2 + t + 1)
                nc.gpsimd.tensor_tensor(out=VA[:, t, :], in0=VA[:, t, :], in1=ROWS[:, 0, :], op=ALU.mult)\
                    .then_inc(S["sg_mul"], 1)
                pool.wait_ge(S["sg_mul"], t + 1)
                nc.gpsimd.tensor_tensor(out=VA[:, t, :], in0=VA[:, t, :], in1=ROWS[:, 1, :], op=ALU.add)\
                    .then_inc(S["sg_v"], 1)

            def picks(p, b, first=False):
                if not first:
                    pool.wait_ge(S["s_mm"], QB * (HB + 2 * p + b - 1))
                for out, sign in ((NPICK[b], -1.0), (PPICK[b], 1.0)):
                    nc.gpsimd.tensor_scalar(out[:, :], ONES[:, 0:out.shape[1]], sign, column(PICK, 2 * p + b),
                                            ALU.mult, ALU.mult).then_inc(S["npick"], 1)

            pool.wait_ge(S["f2_set"], 3)
            for b in range(2):
                picks(0, b, True)
            for p in range(PAIRS - 1):
                for b in range(2):
                    softmax_norm(HB + 2 * p + b)
                    picks(p + 1, b)
            for b in range(2):
                softmax_norm(HB + 2 * (PAIRS - 1) + b)

        @block.scalar
        def _(act):
            def stat_square(n, k):
                act.wait_ge(S["ct"], KT * n + k + 1)
                act.wait_ge(S["sum2"], KT * (n - 1) + k)
                nc.scalar.activation(SQ[:, :], CT[:, :], ACT.Square).then_inc(S["c_sq"], 1)

            def stat_shift(n):
                act.wait_ge(S["sh_mm"], n + 1)
                nc.scalar.activation(SB[:, :], PS[2][:, :], ACT.Copy, scale=1.0 / P).then_inc(S["sh_b"], 1)

            def norm_end(n):
                if n:
                    act.wait_ge(S["st_v"], 4 * n)
                    nc.scalar.activation(ST[:, 24:28], ST[:, 20:24], ACT.Sqrt).then_inc(S["st_sd"], 1)
                if n == 0:
                    act.wait_ge(S["cols_in"], 32)
                for k in range(KT):
                    buf = NBUF[k % 4]
                    gain, offset = norm_cols(n, k)
                    act.wait_ge(S["n_mul"], KT * n + k + 1)
                    nc.scalar.activation(Y[:, k, :], buf[:, :], ACT.Identity, bias=offset, scale=gain)\
                        .then_inc(S["n_x"], 1)
                    if n == DEPTH:
                        act.wait_ge(S["n_x"], norm_uses(n, k))
                        nc.scalar.activation(SQ2[:, k, :], Y[:, k, :], ACT.Square).then_inc(S["r_sq"], 1)
                    else:
                        nc.scalar.activation(XH[:, k, :], buf[:, :], ACT.Identity, bias=offset, scale=gain)\
                            .then_inc(S["n_x"], 1)

            def norm_cols(n, k):
                if n == 0:
                    return EXT[:, E_G + k:E_G + k + 1], EXT[:, E_B + k:E_B + k + 1]
                return col(n - 1, C_LG + k), col(n - 1, C_LB + k)

            def split(l, s, units=(0, 1), i=0):
                split_hi(act, l, s, units, i)

            act.wait_ge(S["ang"], 1)
            nc.scalar.activation(CS[:, :], T0[:, :], ACT.Sin).then_inc(S["cs_done"], 1)
            stat_shift(0)
            for k in range(KT):
                act.wait_ge(S["ct"], k + 1)
                nc.scalar.activation(SQ2[:, k, :], Y[:, k, :], ACT.Square).then_inc(S["c_sq"], 1)
            for s in range(2):
                split(0, s)
            act.wait_ge(S["emb_v"], 4)
            nc.scalar.activation(A2[:, :], A2[:, :], ACT.Sqrt).then_inc(S["emb_sd"], 1)
            norm_end(0)

            def layer(l):
                def evac(m, dst, func):
                    split(l, m + 2)
                    act.wait_ge(w_used, step_done(l, m))
                    return nc.scalar.activation(dst, PS[m % 2][:, :], func)

                for i in range(6):
                    m = T_KV + i
                    split(l, m + 2)
                    act.wait_ge(w_used, step_done(l, m))
                    nc.scalar.activation(LAT[:, i, :], PS[m % 2][:, :], ACT.Copy).then_inc(S["lat_hi"], 1)
                    if i == 2:
                        act.wait_ge(S["lat_bc"], 2 * l + 1)
                    if i >= 1:
                        act.wait_ge(S["sq_sum"], 4 * l + (0, 0, 1, 1, 2, 3)[i])
                    first = i in (0, 2)
                    nc.scalar.activation((T0 if first else Y1)[:, :], PS[m % 2][:, :], ACT.Square)\
                        .then_inc(S["in_ev"], 1)
                    if i == 2:
                        act.wait_ge(S["cond_in"], 16 * (l + 1))
                        nc.scalar.activation(CONDB[:, :], CONDB[:, :], ACT.Silu).then_inc(S["cond_silu"], 1)
                    if i == 1:
                        lat_sd(l, 0)
                split(l, T_KR + 2, (0,))
                lat_sd(l, 1)
                split(l, T_KR + 2, (1,))
                for j in range(GROUPS):
                    m = T_POOL + 2 * j
                    evac(m, G[:, 8 + j, :], ACT.Silu).then_inc(S["in_ev"], 1)
                    if j == 0:
                        act.wait_ge(S["rope_k"], 4 * (l + 1))
                    evac(m + 1, T0[:, :], ACT.Copy).then_inc(S["in_ev"], 1)
                for j in range(GROUPS):
                    m = T_CONV + 4 * j
                    act.wait_ge(S["conv_ev"], GROUPS * l + j)
                    if j == 0:
                        act.wait_ge(S["pool_step"], 32 * (l + 1))
                    evac(m, T0[:, :], ACT.Copy).then_inc(S["in_ev"], 1)
                    if j == 0:
                        act.wait_ge(S["pool_mm"], GROUPS * (l + 1))
                    evac(m + 1, Y1[:, :], ACT.Copy).then_inc(S["in_ev"], 1)
                    split(l, m + 4)
                    act.wait_ge(S["conv_step"], 5 * (GROUPS * l + j) + 1)
                    act.wait_ge(w_used, step_done(l, m + 2))
                    nc.scalar.activation(Y1[:, :], PS[m % 2][:, :], ACT.Copy).then_inc(S["in_ev"], 1)
                    evac(m + 3, G[:, 12 + j, :], ACT.Silu).then_inc(S["in_ev"], 1)
                for j in range(8):
                    if j == 0:
                        act.wait_ge(S["ada_done"], ADA_LAYER * (l + 1))
                    if j < 7:
                        evac(T_GATE + j, G[:, j, :], ACT.Silu).then_inc(S["in_ev"], 1)
                split(l, T_GATE + 9, (0,))
                act.wait_ge(w_used, step_done(l, IN_TILES - 1))
                act.wait_ge(S["lat_n"], 6 * (l + 1))
                for k, i in LAT_TILES:
                    nc.scalar.activation(XH[:, k, :], LAT[:, i, :], ACT.Copy).then_inc(S["krh"], 1)
                act.wait_ge(S["rope_k"], 4 * l + 4)
                nc.scalar.activation(XL[0:ROPE, 14, :], LAT[0:ROPE, 6, :], ACT.Copy).then_inc(S["krh"], 1)
                act.wait_ge(S["krh"], 8 * l + 7)
                nc.scalar.activation(XH[ROPE:P, 14, :], XL[0:ROPE, 14, :].bitcast(F32), ACT.Copy)\
                    .then_inc(S["krh"], 1)
                nc.scalar.activation(G[:, 7, :], PS[(T_GATE + 7) % 2][:, :], ACT.Silu).then_inc(S["in_ev"], 1)

                for h in range(HEADS):
                    hh = HEADS * l + h
                    if h == 0:
                        act.wait_ge(S["krl"], l + 1)
                    act.wait_ge(S["proj"], 2 * hh + 2)
                    act.wait_ge(S["s_mm"], QB * hh)
                    nc.scalar.activation(XH[:, 15, :], PS[2][:, :], ACT.Copy).then_inc(S["kn_hi"], 1)
                    if h:
                        pt_hi(hh - 1, 0)
                    act.wait_ge(S["rope_q"], 5 * hh + 4)
                    nc.scalar.activation(QR[0:ROPE, :], TR[0:ROPE, :], ACT.Copy).then_inc(S["qr_hi"], 1)
                    if h:
                        pt_hi(hh - 1, 1)
                        pt_hi(hh - 1, 2)
                    split(l, IN_TILES + h + 1, (1,))
                    split(l, IN_TILES + h + 2, (0,))
                    act.wait_ge(w_used, step_done(l, IN_TILES + h))
                    nc.scalar.activation(QNH[:, :], PS[0][:, :], ACT.Copy).then_inc(S["qn_hi"], 1)
                    if h:
                        pt_hi(hh - 1, 3)
                    softmax_exp(hh, 0, MLA_SCALE)
                    act.wait_ge(S["pv_mm"], QB * hh)
                    nc.scalar.activation(VSH[:, :, :], PS[3][:, :].rearrange("p (t d) -> p t d", t=QB), ACT.Copy)\
                        .then_inc(S["v_hi"], 1)
                    for i in range(1, QB):
                        softmax_exp(hh, i, MLA_SCALE)
                    if h:
                        to_mix(l, h - 1)
                split(l, T_OUT + 1, (1,))
                for n, i in ((7, 0), (8, 1), (9, None), (10, 2), (11, None), (12, 3), (13, None), (14, None), (15, None)):
                    to_mix(l, n)
                    if i is not None:
                        pt_hi(HEADS * l + HEADS - 1, i)
                def out_stat(m, i=0):
                    if m < KT - 1:
                        split(l, T_OUT + m + 2, (0,), i)
                    if m == 1:
                        stat_shift(l + 1)
                        stat_square(l + 1, 0)
                    if m >= 1:
                        stat_square(l + 1, m + 2 * i)
                    if m < KT - 2:
                        split(l, T_OUT + m + 2, (1,), i)

                out_stat(0)
                out_stat(1)
                with act.Fori(0, KT // 2 - 2) as i:
                    out_stat(2, i)
                    out_stat(3, i)
                out_stat(KT - 2)
                out_stat(KT - 1)
                split(l, T_OUT + KT, (1,))
                split(l, T_OUT + KT + 1)
                norm_end(l + 1)

            def lat_sd(l, q):
                act.wait_ge(S["lat_v"], 2 * l + q + 1)
                nc.scalar.activation(ST[:, 24:28], ST[:, 20:24], ACT.Sqrt).then_inc(S["lat_sd"], 1)

            def pt_hi(hh, i):
                act.wait_ge(S["p_tr"], QB * hh + i + 1)
                act.wait_ge(S["pv_mm"], QB * hh + max(i - 1, 0))
                nc.scalar.activation(PTH[i % 2][:, :P * (i + 1)], PS[6 + i % 2][:, :P * (i + 1)], ACT.Copy)\
                    .then_inc(S["pt_hi"], 1)

            def softmax_exp(hh, i, scale):
                act.wait_ge(S["s_nb"], QB * hh + i + 1)
                act.wait_ge(S["p_tr"], QB * hh)
                nc.scalar.activation(PR[:, poff(i):poff(i + 1)], PS[5 - i % 2][:, :P * (i + 1)], ACT.Exp,
                                     bias=ST[:, 4 + i:5 + i], scale=scale,
                                     accum_out=ST[:, 8 + i:9 + i]).then_inc(S["s_exp"], 1)

            def to_mix(l, n):
                k = MIX_ORDER[n]
                if k < 8:
                    act.wait_ge(S["pv_out"], HEADS * l + k + 1)
                elif k < 14:
                    act.wait_ge(w_used, step_done(l, T_OUT - 1))
                else:
                    act.wait_ge(S["s_mm"], QB * HEADS * (l + 1))
                nc.scalar.activation(XH[:, k, :], G[:, k, :], ACT.Copy).then_inc(S["mix_hi"], 1)

            for l in range(DEPTH):
                layer(l)

            def rms_sd(r):
                act.wait_ge(S["r_v"], r + 1)
                nc.scalar.activation(ST[:, 24:28], ST[:, 20:24], ACT.Sqrt).then_inc(S["r_sd"], 1)

            def half_split(s, n, i=0):
                split_hi(act, B2, s, (n,), i)

            act.wait_ge(S["r_v"], 1)
            nc.scalar.activation(A2[:, :], A2[:, :], ACT.Sqrt).then_inc(S["r_sd"], 1)
            for k in range(KT):
                act.wait_ge(S["h_mul"], k + 1)
                nc.scalar.activation(XH[:, k, :], H32[:, k, :], ACT.Identity, bias=MOD[:, k:k + 1])\
                    .then_inc(S["h_hi"], 1)
            for s in range(T2_F):
                j = s % 8
                split(B2, s + 2)
                act.wait_ge(w_used, step_done(B2, s))
                if s < T2_U:
                    if j >= 2:
                        act.wait_ge(S["va_tr"], j - 1)
                    nc.scalar.activation((T0, Y1)[j % 2][:, :], PS[s % 2][:, :], ACT.Gelu).then_inc(S["in2_ev"], 1)
                elif s < T2_GA:
                    nc.scalar.activation(G[:, j, :], PS[s % 2][:, :], ACT.Gelu).then_inc(S["in2_ev"], 1)
                else:
                    if j >= 2:
                        act.wait_ge(S["ga_ev"], j - 1)
                    nc.scalar.activation((T0, Y1)[j % 2][:, :], PS[s % 2][:, :], ACT.Silu).then_inc(S["in2_ev"], 1)
                if s == T2_U:
                    act.wait_ge(S["bn_set"], 3 * QB + 1)
                    nc.scalar.activation(ST[:, 24:28], ST[:, 20:24], ACT.Sqrt).then_inc(S["sg_sd"], 1)
            split(B2, T2_F + 2)
            act.wait_ge(S["f_step"], 3)
            nc.scalar.activation(Y1[0:16, :], Y1[0:16, :], ACT.Exp).then_inc(S["f_act"], 1)
            act.wait_ge(S["f_step"], 4)
            nc.scalar.activation(TV[0:16, :], U[0:16, 0:NT], ACT.Ln).then_inc(S["f_act"], 1)

            def q_hi(p, first):
                act.wait_ge(w_used, step_done(B2, T2_PAIR, 2 * p))
                act.wait_ge(S["s_mm"], QB * (HB + 2 * p))
                if first:
                    act.wait_ge(S["sg_mm"], A_HEADS)
                nc.scalar.activation(QNH[:, :], PS[1][:, :], ACT.Copy, scale=Q2_SCALE).then_inc(S["qn_hi"], 1)

            def gate(p):
                act.wait_ge(w_used, step_done(B2, T2_PAIR + 3, 2 * p))
                act.wait_ge(S["sg_out"], A_HEADS)
                nc.scalar.activation(feature(G, 8 + p), PS[0][:, :], ACT.Silu).then_inc(S["in2_ev"], 1)

            def pair(p, first):
                s, a, i = T2_PAIR, HB + 2 * p, 2 * p
                if not first:
                    gate(p - 1)
                    softmax_exp(a - 1, 3, 1.0)
                    pt_hi(a - 1, 0)
                    pt_hi(a - 1, 1)
                    pt_hi(a - 1, 2)
                    pt_hi(a - 1, 3)
                half_split(s + 2, 0, i)
                half_split(s + 2, 1, i)
                if first:
                    act.wait_ge(S["f_step"], 11)
                    act.wait_ge(S["f2_set"], 1)
                    for r in (0, 64):
                        nc.scalar.activation(F2[r:r + 16, :], Y1[0:16, :], ACT.Copy).then_inc(S["f2_hi"], 1)
                    half_split(s + 3, 0, i)
                q_hi(p, first)
                if not first:
                    half_split(s + 3, 0, i)
                half_split(s + 3, 1, i)
                act.wait_ge(w_used, step_done(B2, s + 1, i))
                nc.scalar.activation(KH[:, :], PS[0][:, :], ACT.Copy).then_inc(S["kn_hi"], 1)
                softmax_exp(a, 0, 1.0)
                softmax_exp(a, 1, 1.0)
                half_split(s + 4, 0, i)
                softmax_exp(a, 2, 1.0)
                softmax_exp(a, 3, 1.0)
                half_split(s + 4, 1, i)
                act.wait_ge(w_used, step_done(B2, s + 2, i))
                if not first:
                    act.wait_ge(S["v_tr"], p)
                nc.scalar.activation(TV[:, :], PS[1][:, :], ACT.Copy).then_inc(S["v_out"], 1)
                pt_hi(a, 0)
                act.wait_ge(S["v_tr"], p + 1)
                act.wait_ge(S["pv_mm"], QB * a)
                nc.scalar.activation(VSH[:, :, :], PS[3][:, :].rearrange("p (t d) -> p t d", t=QB), ACT.Copy)\
                    .then_inc(S["v_hi"], 1)
                pt_hi(a, 1)
                pt_hi(a, 2)
                pt_hi(a, 3)
                half_split(s + 5, 0, i)
                softmax_exp(a + 1, 0, 1.0)
                softmax_exp(a + 1, 1, 1.0)
                half_split(s + 5, 1, i)
                softmax_exp(a + 1, 2, 1.0)

            pair(0, True)
            with act.Fori(1, PAIRS) as p:
                pair(p, False)
            last = HB + B2_HEADS - 1

            def mix2(k):
                if k >= 8:
                    act.wait_ge(S["pv_out"], HB + 2 * (k - 7))
                nc.scalar.activation(XH[:, k, :], G[:, k, :], ACT.Copy).then_inc(S["mix_hi"], 1)

            for k in range(3):
                mix2(k)
            gate(PAIRS - 1)
            softmax_exp(last, 3, 1.0)
            for i in range(QB):
                for k in MIX_BEHIND[i]:
                    mix2(k)
                pt_hi(last, i)
            half_split(T2_OUT + 2, 0)
            mix2(15)
            half_split(T2_OUT + 2, 1)
            def out_square(m, i=0):
                if m:
                    half_split(T2_OUT + m + 2, 0, i)
                act.wait_ge(S["out2_ev"], m + 1 + 2 * i)
                act.wait_ge(S["r_sum"], m + 2 * i)
                nc.scalar.activation(SQ[:, :], feature(Y, m + 2 * i), ACT.Square).then_inc(S["r_sq"], 1)
                if m:
                    half_split(T2_OUT + m + 2, 1, i)

            out_square(0)
            out_square(1)
            with act.Fori(0, KT // 2 - 2) as i:
                out_square(2, i)
                out_square(3, i)
            out_square(KT - 2)
            out_square(KT - 1)
            rms_sd(1)

        @block.vector
        def _(dve):
            V = nc.vector
            TT, TS, STT = V.tensor_tensor, V.tensor_scalar, V.scalar_tensor_tensor

            def split(l, s, units=(0, 1), i=0):
                split_lo(dve, l, s, units, i)
                if l < B2 and 5 <= s <= T_GATE + 1 and units[-1] == 1:
                    for n in range(ADA_LAYER * (s - 5) // (T_GATE - 3), ADA_LAYER * (s - 4) // (T_GATE - 3)):
                        ada(l, n)

            def ada(l, n):
                g = ADA_LAYER * l + n
                if n == 0:
                    dve.wait_ge(S["cond_silu"], l + 1)
                dve.wait_ge(S[f"ada_in{n % 2}"], 16 * (g // 2 + 1))
                STT(out=ADAB[:, n % 2, :], in0=ADAB[:, n % 2, :], scalar=1.0,
                    in1=CONDB[:, (n % 2) * UNIT:(n % 2 + 1) * UNIT], op0=ALU.mult, op1=ALU.mult,
                    accum_out=MODP[:, g:g + 1]).then_inc(S["ada_done"], 1)

            for t in range(16):
                V.memset(RC[:, t:t + 1], 1.0 / (t + 1))
            posf, turns = T0, Y1
            dve.wait_ge(S["const_in"], 32)
            n = 0

            def rot(ins):
                nonlocal n
                n += 1
                ins.then_inc(S["rng"], 1)
                dve.wait_ge(S["rng"], n)

            rot(V.tensor_copy(posf[:, :], CS[:, :].bitcast(I32)))
            rot(TS(posf[:, :], posf[:, :], ST[:, 0:1], None, ALU.mult))
            ROUND = 12582912.0
            rot(TS(turns[:, :], posf[:, :], 1.0 / TWO_PI, ST[:, 1:2], ALU.mult, ALU.add))
            rot(TS(turns[:, :], turns[:, :], ROUND, -ROUND, ALU.add, ALU.add))
            part1 = 6.28125
            part2 = float((np.float32(TWO_PI - part1).view(np.uint32) & np.uint32(0xFFFFF000)).view(np.float32))
            part3 = float(TWO_PI - part1 - part2)
            for part in (part1, part2, part3):
                rot(STT(out=posf[:, :], in0=turns[:, :], scalar=-part, in1=posf[:, :], op0=ALU.mult, op1=ALU.add))
            rot(TS(posf[:, :], posf[:, :], ST[:, 2:3], PI_BELOW, ALU.add, ALU.min))
            TS(posf[:, :], posf[:, :], -PI_BELOW, None, ALU.max).then_inc(S["ang"], 1)

            def stat(n, k):
                if isinstance(k, int) and k == 0:
                    dve.wait_ge(S["sh_b"], n + 1)
                dve.wait_ge(S["c_sq"], KT * n + k)
                dve.wait_ge(S["sum1"], KT * (n - 1) + k)
                TT(out=CT[:, :], in0=feature(Y, k), in1=SB[:, :], op=ALU.subtract).then_inc(S["ct"], 1)
                dve.wait_ge(S["ct"], KT * n + k + 1)
                TT(out=A1[:, :], in0=A1[:, :], in1=CT[:, :], op=ALU.add).then_inc(S["sum1"], 1)
                dve.wait_ge(S["c_sq"], KT * n + k + 1)
                dve.wait_ge(S["sum2"], KT * (n - 1) + k)
                TT(out=A2[:, :], in0=A2[:, :], in1=SQ[:, :], op=ALU.add).then_inc(S["sum2"], 1)

            def rms_sum(k):
                dve.wait_ge(S["r_sq"], KT + k + 1)
                if isinstance(k, int) and k == 0:
                    V.tensor_copy(A1[:, :], SQ[:, :]).then_inc(S["r_sum"], 1)
                else:
                    dve.wait_ge(S["r_sum"], k)
                    TT(out=A1[:, :], in0=A1[:, :], in1=SQ[:, :], op=ALU.add).then_inc(S["r_sum"], 1)

            def rms_end():
                dve.wait_ge(S["r_mm"], 2)
                TS(ST[:, 20:24], PS[3][:, 0:4], 1.0 / D, RMS_EPS, ALU.mult, ALU.add).then_inc(S["r_v"], 1)
                dve.wait_ge(S["r_sd"], 2)
                V.reciprocal(ST[:, 28:32], ST[:, 24:28]).then_inc(S["r_ri"], 1)
                dve.wait_ge(S["r_ri"], 2)
                for t in range(QB):
                    TS(DG[1][:, t, :], IDN[:, :], ST[:, 28 + t:29 + t], None, ALU.mult).then_inc(S["r_dg"], 1)
                dve.wait_ge(S["r_bc"], 1)

            def emb_end():
                dve.wait_ge(S["emb_mm"], 1)
                TS(SB[:, :], PS[3][:, :], 1.0 / D, None, ALU.mult).then_inc(S["emb_v"], 1)
                dve.wait_ge(S["emb_v"], 1)
                TT(out=A1[:, :], in0=SB[:, :], in1=SB[:, :], op=ALU.mult).then_inc(S["emb_v"], 1)
                dve.wait_ge(S["emb_v"], 2)
                STT(out=A2[:, :], in0=PS[7][:, :], scalar=1.0 / D, in1=A1[:, :], op0=ALU.mult, op1=ALU.subtract)\
                    .then_inc(S["emb_v"], 1)
                dve.wait_ge(S["emb_v"], 3)
                TS(A2[:, :], A2[:, :], LN_EPS, None, ALU.add).then_inc(S["emb_v"], 1)
                dve.wait_ge(S["emb_sd"], 1)
                V.reciprocal(PS[7][:, :], A2[:, :]).then_inc(S["sh_tot"], 1)
                dve.wait_ge(S["sh_tot"], 1)

            def norm_end(n):
                dve.wait_ge(S["st_mm"], n)
                TS(ST[:, 16:24], PS[3][:, 0:8], 1.0 / D, None, ALU.mult).then_inc(S["st_v"], 1)
                dve.wait_ge(S["st_v"], 4 * n - 3)
                TT(out=ST[:, 28:32], in0=ST[:, 16:20], in1=ST[:, 16:20], op=ALU.mult).then_inc(S["st_v"], 1)
                dve.wait_ge(S["st_v"], 4 * n - 2)
                TT(out=ST[:, 20:24], in0=ST[:, 20:24], in1=ST[:, 28:32], op=ALU.subtract).then_inc(S["st_v"], 1)
                dve.wait_ge(S["st_v"], 4 * n - 1)
                TS(ST[:, 20:24], ST[:, 20:24], LN_EPS, None, ALU.add).then_inc(S["st_v"], 1)
                for t in range(QB):
                    TS(DG[0][:, t, :], IDN[:, :], ST[:, 16 + t:17 + t], None, ALU.mult).then_inc(S["dg_m"], 1)
                dve.wait_ge(S["st_sd"], n)
                V.reciprocal(ST[:, 28:32], ST[:, 24:28]).then_inc(S["st_ri"], 1)
                dve.wait_ge(S["st_ri"], n)
                for t in range(QB):
                    TS(DG[1][:, t, :], IDN[:, :], ST[:, 28 + t:29 + t], None, ALU.mult).then_inc(S["dg_r"], 1)
                dve.wait_ge(S["bc_m"], n)
                TT(out=SB[:, :], in0=SB[:, :], in1=PS[2][:, :], op=ALU.add).then_inc(S["sh_tot"], 1)
                dve.wait_ge(S["bc_r"], n)

            def normalise(n):
                def lo(k):
                    dve.wait_ge(S["n_x"], norm_uses(n, k))
                    TT(out=XL[:, k, :], in0=Y[:, k, :], in1=XH[:, k, :].bitcast(F32), op=ALU.subtract)\
                        .then_inc(S["x_lo_s"], 1)

                for k in range(KT):
                    buf = NBUF[k % 4]
                    dve.wait_ge(S["n_sub"], KT * n + k + 1)
                    TT(out=buf[:, :], in0=buf[:, :], in1=PS[7][:, :], op=ALU.mult).then_inc(S["n_mul"], 1)
                    if k >= 2 and n < DEPTH:
                        lo(k - 2)
                if n < DEPTH:
                    lo(KT - 2)
                    lo(KT - 1)

            dve.wait_ge(S["sh_b"], 1)
            for k in range(KT):
                dve.wait_ge(xt_in[k // 2], 32)
                TT(out=Y[:, k, :], in0=Y[:, k, :], in1=SB[:, :], op=ALU.subtract).then_inc(S["ct"], 1)
            for s in range(2):
                split(0, s)
            emb_end()
            normalise(0)

            def rope(src, cnt, base):
                TT(out=TR[0:ROPE, :], in0=src[0:ROPE, :], in1=CS[0:ROPE, :], op=ALU.mult).then_inc(cnt, 1)
                TT(out=src[64:96, :], in0=src[32:64, :], in1=CS[96:128, :], op=ALU.mult).then_inc(cnt, 1)
                TT(out=src[96:128, :], in0=src[0:32, :], in1=CS[64:96, :], op=ALU.mult).then_inc(cnt, 1)
                dve.wait_ge(cnt, base + 3)
                return TR[0:ROPE, :], src[64:128, :]

            def layer(l):
                def pool_group(j):
                    w = 2 << j
                    step = 32 * l + (0, 5, 12, 21)[j]
                    src = T0
                    for d in range(j + 1):
                        dst, sh = (Y1, U)[d % 2], 1 << d
                        V.tensor_copy(dst[:, 0:sh], src[:, 0:sh]).then_inc(S["pool_step"], 1)
                        TT(out=dst[:, sh:NT], in0=src[:, sh:NT], in1=src[:, 0:NT - sh], op=ALU.add)\
                            .then_inc(S["pool_step"], 1)
                        step += 2
                        dve.wait_ge(S["pool_step"], step)
                        src = dst
                    z = (U, Y1)[j % 2]
                    STT(out=z[:, w - 1:NT], in0=src[:, w - 1:NT], scalar=1.0 / w, in1=T0[:, w - 1:NT],
                        op0=ALU.mult, op1=ALU.subtract).then_inc(S["pool_step"], 1)
                    TT(out=ST[:, 16:16 + w - 1], in0=src[:, 0:w - 1], in1=RC[:, 0:w - 1], op=ALU.mult)\
                        .then_inc(S["pool_step"], 1)
                    dve.wait_ge(S["pool_step"], step + 2)
                    TT(out=z[:, 0:w - 1], in0=ST[:, 16:16 + w - 1], in1=T0[:, 0:w - 1], op=ALU.subtract)\
                        .then_inc(S["pool_step"], 1)
                    dve.wait_ge(S["pool_step"], step + 3)

                def pool_out(j):
                    dve.wait_ge(S["pool_mm"], GROUPS * l + j + 1)
                    STT(out=G[:, 8 + j, :], in0=PS[4][:, :], scalar=col(l, C_PS + j), in1=G[:, 8 + j, :],
                        op0=ALU.mult, op1=ALU.mult).then_inc(S["pool_ev"], 1)

                def lat_norm(q):
                    n = 2 * l + q
                    dve.wait_ge(S["lat_mm"], n + 1)
                    TS(ST[:, 20:24], PS[5][:, 0:4], 1.0 / (KV_LORA, Q_LORA)[q], RMS_EPS, ALU.mult, ALU.add)\
                        .then_inc(S["lat_v"], 1)
                    dve.wait_ge(S["lat_sd"], n + 1)
                    V.reciprocal(ST[:, 28:32], ST[:, 24:28]).then_inc(S["lat_ri"], 1)
                    dve.wait_ge(S["lat_ri"], n + 1)
                    for t in range(QB):
                        TS(T0[:, t * P:(t + 1) * P], IDN[:, :], ST[:, 28 + t:29 + t], None, ALU.mult)\
                            .then_inc(S["lat_dg"], 1)

                def lat_apply(q):
                    dve.wait_ge(S["lat_bc"], 2 * l + q + 1)
                    for i in ((0, 1), (2, 3, 4, 5))[q]:
                        g = col(l, C_KVG + i if q == 0 else C_QG + i - 2)
                        STT(out=LAT[:, i, :], in0=LAT[:, i, :], scalar=g, in1=PS[6][:, :], op0=ALU.mult,
                            op1=ALU.mult).then_inc(S["lat_n"], 1)

                sums = 0
                for i in range(6):
                    m = T_KV + i
                    split(l, m + 2)
                    if i not in (0, 2):
                        dve.wait_ge(S["in_ev"], taken(l, m))
                        dve.wait_ge(S["sq_sum"], 4 * l + sums)
                        TT(out=T0[:, :], in0=T0[:, :], in1=Y1[:, :], op=ALU.add).then_inc(S["sq_sum"], 1)
                        sums += 1
                    if i == 1:
                        lat_norm(0)
                    if i == 2:
                        lat_apply(0)
                split(l, T_KR + 2, (0,))
                lat_norm(1)
                split(l, T_KR + 2, (1,))
                lat_apply(1)
                dve.wait_ge(w_used, step_done(l, T_KR))
                dve.wait_ge(S["lat_dg"], 8 * (l + 1))
                a, b = rope(PS[7], S["rope_k"], 4 * l)
                TT(out=LAT[0:ROPE, 6, :], in0=a, in1=b, op=ALU.add).then_inc(S["rope_k"], 1)
                for j in range(GROUPS):
                    m = T_POOL + 2 * j
                    split(l, m + 2)
                    split(l, m + 3)
                    if j:
                        pool_out(j - 1)
                    dve.wait_ge(S["in_ev"], taken(l, m + 1))
                    pool_group(j)
                for j in range(GROUPS):
                    m = T_CONV + 4 * j
                    st = 5 * (GROUPS * l + j)
                    cw = lambda tap: col(l, C_CW + TAPS * j + tap)
                    split(l, m + 2)
                    split(l, m + 3)
                    if j == 0:
                        pool_out(GROUPS - 1)
                        V.memset(U[:, 0:TAPS - 1], 0.0).then_inc(S["conv_ready"], 1)
                        dve.wait_ge(S["conv_ready"], l + 1)
                    dve.wait_ge(S["in_ev"], taken(l, m + 1))
                    TT(out=U[:, 2:], in0=T0[:, :], in1=Y1[:, :], op=ALU.mult).then_inc(S["conv_step"], 1)
                    dve.wait_ge(S["conv_step"], st + 1)
                    TS(T0[:, :], U[:, 2:], cw(2), None, ALU.mult).then_inc(S["conv_step"], 1)
                    for tap in (1, 0):
                        dve.wait_ge(S["conv_step"], st + 3 - tap)
                        STT(out=T0[:, :], in0=U[:, tap:tap + NT], scalar=cw(tap), in1=T0[:, :],
                            op0=ALU.mult, op1=ALU.add).then_inc(S["conv_step"], 1)
                    split(l, m + 4)
                    dve.wait_ge(S["conv_step"], st + 4)
                    dve.wait_ge(S["in_ev"], taken(l, m + 2))
                    TT(out=T0[:, :], in0=T0[:, :], in1=Y1[:, :], op=ALU.mult).then_inc(S["conv_step"], 1)
                    split(l, m + 5)
                    dve.wait_ge(S["conv_step"], st + 5)
                    dve.wait_ge(S["in_ev"], taken(l, m + 3))
                    TT(out=G[:, 12 + j, :], in0=G[:, 12 + j, :], in1=T0[:, :], op=ALU.mult).then_inc(S["conv_ev"], 1)
                for m in range(T_GATE, IN_TILES):
                    split(l, m + 2, (0, 1) if m < IN_TILES - 1 else (0,))
                if l == DEPTH - 1:
                    dve.wait_ge(S["ada_done"], ADA_UNITS)
                    TT(out=MOD[:, :], in0=MODP[:, 0::2], in1=MODP[:, 1::2], op=ALU.add).then_inc(S["mod_set"], 1)
                    dve.wait_ge(S["mod_set"], 1)
                    TT(out=MOD[:, :], in0=MOD[:, :], in1=EXT[:, E_BADA:E_BADA + ADA_TILES], op=ALU.add)\
                        .then_inc(S["mod_set"], 1)
                    dve.wait_ge(S["mod_set"], 2)
                    STT(out=NG[:, :], in0=MOD[:, KT:2 * KT], scalar=1.0, in1=EXT[:, E_NG:E_NG + KT],
                        op0=ALU.add, op1=ALU.mult).then_inc(S["mod_set"], 1)
                    dve.wait_ge(S["mod_set"], 3)
                for n, (k, i) in enumerate(LAT_TILES):
                    dve.wait_ge(S["krh"], 8 * l + n + 1)
                    TT(out=XL[:, k, :], in0=LAT[:, i, :], in1=XH[:, k, :].bitcast(F32), op=ALU.subtract)\
                        .then_inc(S["lat_lo"], 1)
                dve.wait_ge(S["krh"], 8 * l + 7)
                TT(out=XH[0:ROPE, 14, :], in0=LAT[0:ROPE, 6, :], in1=XL[0:ROPE, 14, :].bitcast(F32),
                   op=ALU.subtract).then_inc(S["krl"], 1)

                for h in range(HEADS):
                    hh = HEADS * l + h
                    dve.wait_ge(S["proj"], 2 * hh + 1)
                    if h == 0:
                        dve.wait_ge(S["rope_k"], 4 * l + 4)
                    a, b = rope(PS[1], S["rope_q"], 5 * hh)
                    TT(out=a, in0=a, in1=b, op=ALU.add).then_inc(S["rope_q"], 1)
                    dve.wait_ge(S["kn_hi"], hh + 1)
                    TT(out=XL[:, 15, :], in0=PS[2][:, :], in1=XH[:, 15, :].bitcast(F32), op=ALU.subtract)\
                        .then_inc(S["kn_lo"], 1)
                    if h:
                        pt_lo(hh - 1, 0)
                    dve.wait_ge(S["qr_hi"], hh + 1)
                    TT(out=QR[ROPE:P, :], in0=TR[0:ROPE, :], in1=QR[0:ROPE, :].bitcast(F32), op=ALU.subtract)\
                        .then_inc(S["rope_q"], 1)
                    if h:
                        pt_lo(hh - 1, 1)
                        pt_lo(hh - 1, 2)
                    split(l, IN_TILES + h + 1, (1,))
                    split(l, IN_TILES + h + 2, (0,))
                    dve.wait_ge(S["qn_hi"], hh + 1)
                    TT(out=QNL[:, :], in0=PS[0][:, :], in1=QNH[:, :].bitcast(F32), op=ALU.subtract)\
                        .then_inc(S["qn_lo"], 1)
                    if h:
                        pt_lo(hh - 1, 3)
                    row_max(hh, 0, MLA_SCALE)
                    if h:
                        head_out(hh - 1, h - 1)
                    for i in range(1, QB):
                        row_max(hh, i, MLA_SCALE)
                        recip(hh, i - 1)
                    recip(hh, QB - 1)
                    dve.wait_ge(S["v_hi"], hh + 1)
                    TT(out=VSL[:, :, :], in0=PS[3][:, :].rearrange("p (t d) -> p t d", t=QB),
                       in1=VSH[:, :, :].bitcast(F32), op=ALU.subtract).then_inc(S["v_lo"], 1)
                    if h:
                        to_mix(l, h - 1)
                split(l, T_OUT + 1, (1,))
                for n, i in ((7, 0), (8, 1), (9, None), (10, 2), (11, None), (12, 3), (13, None), (14, None)):
                    to_mix(l, n)
                    if i is not None:
                        pt_lo(HEADS * l + HEADS - 1, i)
                head_out(HEADS * l + HEADS - 1, HEADS - 1)
                to_mix(l, KT - 1)

                def out_tile(m, i=0):
                    if m < KT - 1:
                        split(l, T_OUT + m + 2, (0,), i)
                    dve.wait_ge(w_used, step_done(l, T_OUT + m, i))
                    if m == 0:
                        dve.wait_ge(S["res"], KT * (l + 1))
                    y = feature(Y, m + 2 * i)
                    TT(out=y, in0=y, in1=PS[m % 2][:, :], op=ALU.add).then_inc(S["out_ev"], 1)
                    if m == 1:
                        dve.wait_ge(S["zero"], 2 * (l + 1))
                        stat(l + 1, 0)
                    if m >= 1:
                        dve.wait_ge(S["out_ev"], KT * l + m + 1 + 2 * i)
                        stat(l + 1, m + 2 * i)
                    if m < KT - 2:
                        split(l, T_OUT + m + 2, (1,), i)

                out_tile(0)
                out_tile(1)
                with dve.Fori(0, KT // 2 - 2) as i:
                    out_tile(2, i)
                    out_tile(3, i)
                out_tile(KT - 2)
                out_tile(KT - 1)
                split(l, T_OUT + KT, (1,))
                split(l, T_OUT + KT + 1)
                norm_end(l + 1)
                normalise(l + 1)

            def pt_lo(hh, i):
                dve.wait_ge(S["pt_hi"], QB * hh + i + 1)
                TT(out=PTL[i % 2][:, :P * (i + 1)], in0=PS[6 + i % 2][:, :P * (i + 1)],
                   in1=PTH[i % 2][:, :P * (i + 1)].bitcast(F32), op=ALU.subtract).then_inc(S["pt_lo"], 1)

            def head_out(hh, h):
                dve.wait_ge(S["pv_mm"], QB * (hh + 1))
                TT(out=G[:, h, :], in0=PS[2][:, :], in1=G[:, h, :], op=ALU.mult).then_inc(S["pv_out"], 1)

            def recip(hh, i):
                dve.wait_ge(S["s_exp"], QB * hh + i + 1)
                V.reciprocal(ST[:, 12 + i:13 + i], ST[:, 8 + i:9 + i]).then_inc(S["s_rc"], 1)

            def row_max(hh, i, scale):
                dve.wait_ge(S["s_mm"], QB * hh + i + 1)
                if i == 0:
                    dve.wait_ge(S["p_norm"], QB * hh)
                V.reduce_max(ST[:, i:i + 1], PS[5 - i % 2][:, :P * (i + 1)], axis=AXX).then_inc(S["s_max"], 1)
                dve.wait_ge(S["s_max"], QB * hh + i + 1)
                TS(ST[:, 4 + i:5 + i], ST[:, i:i + 1], -scale, None, ALU.mult).then_inc(S["s_nb"], 1)

            def to_mix(l, n):
                k = MIX_ORDER[n]
                dve.wait_ge(S["mix_hi"], KT * l + n + 1)
                TT(out=XL[:, k, :], in0=G[:, k, :], in1=XH[:, k, :].bitcast(F32), op=ALU.subtract)\
                    .then_inc(S["mix_lo"], 1)

            for l in range(DEPTH):
                layer(l)

            def h_lo(k):
                dve.wait_ge(S["h_hi"], k + 1)
                STT(out=XL[:, k, :], in0=H32[:, k, :], scalar=MOD[:, k:k + 1], in1=XH[:, k, :].bitcast(F32),
                    op0=ALU.add, op1=ALU.subtract).then_inc(S["x_lo_s"], 1)

            dve.wait_ge(S["r_mm"], 1)
            TS(A2[:, :], PS[6][:, :], 1.0 / D, RMS_EPS, ALU.mult, ALU.add).then_inc(S["r_v"], 1)
            dve.wait_ge(S["r_sd"], 1)
            V.reciprocal(A2[:, :], A2[:, :]).then_inc(S["r_ri"], 1)
            dve.wait_ge(S["r_ri"], 1)
            for k in range(KT):
                STT(out=H32[:, k, :], in0=Y[:, k, :], scalar=NG[:, k:k + 1], in1=A2[:, :], op0=ALU.mult,
                    op1=ALU.mult).then_inc(S["h_mul"], 1)
                if k:
                    h_lo(k - 1)
            h_lo(KT - 1)

            def va_out(j):
                dve.wait_ge(S["va_tr"], j + 1)
                V.tensor_copy(VA[:, :, j * P:(j + 1) * P], PS[2 + j % 2][:, :].rearrange("p (t d) -> p t d", t=QB))\
                    .then_inc(S["va_ev"], 1)

            def va_norm():
                dve.wait_ge(S["va_ev"], A_HEADS)
                for t in range(QB):
                    for c in range(2):
                        V.bn_stats(BN[:, t, c, :], VA[:, t, c * NT:(c + 1) * NT]).then_inc(S["bn_set"], 1)
                dve.wait_ge(S["bn_set"], 2 * QB)
                for t in range(QB):
                    V.bn_aggr(MV[:, t, :], BN[:, t, :, :]).then_inc(S["bn_set"], 1)
                dve.wait_ge(S["bn_set"], 3 * QB)
                TS(ST[:, 20:24], MV[:, :, 1], RMS_EPS, None, ALU.add).then_inc(S["bn_set"], 1)
                split(B2, T2_U + 3)
                dve.wait_ge(S["sg_sd"], 1)
                V.reciprocal(ST[:, 28:32], ST[:, 24:28]).then_inc(S["bn_set"], 1)
                dve.wait_ge(S["bn_set"], 3 * QB + 2)
                for t in range(QB):
                    TS(VA[:, t, :], VA[:, t, :], MV[:, t, 0:1], ST[:, 28 + t:29 + t], ALU.subtract, ALU.mult)\
                        .then_inc(S["bn_set"], 1)

            for s in range(T2_F):
                if s != T2_U + 1:
                    split(B2, s + 2)
                j = s % 8
                if s == 2:
                    va_out(0)
                if 2 <= s <= T2_U:
                    va_out(s - 1)
                if s == T2_U:
                    va_norm()
                if s >= T2_GA:
                    dve.wait_ge(S["in2_ev"], s + 1)
                    TT(out=G[:, j, :], in0=G[:, j, :], in1=(T0, Y1)[j % 2][:, :], op=ALU.mult).then_inc(S["ga_ev"], 1)
            split(B2, T2_F + 2)
            fx, fe, fw, fl = T0[0:16, :], Y1[0:16, :], U[0:16, 0:NT], TV[0:16, :]
            dve.wait_ge(w_used, step_done(B2, T2_F))
            dve.wait_ge(S["ga_ev"], A_HEADS)
            TS(fx, PS[6][0:16, :], EXT[0:16, E_BF:E_BF + 1], None, ALU.add).then_inc(S["f_step"], 1)
            dve.wait_ge(S["f_step"], 1)
            TS(fe, fx, -1.0, None, ALU.mult).then_inc(S["f_step"], 1)
            dve.wait_ge(S["f_step"], 2)
            TT(out=fe, in0=fe, in1=fx, op=ALU.min).then_inc(S["f_step"], 1)
            dve.wait_ge(S["f_act"], 1)
            TS(fw, fe, 1.0, None, ALU.add).then_inc(S["f_step"], 1)
            TS(fx, fx, 0.0, None, ALU.min).then_inc(S["f_step"], 1)
            dve.wait_ge(S["f_step"], 4)
            STT(out=fe, in0=fw, scalar=-1.0, in1=fe, op0=ALU.add, op1=ALU.subtract).then_inc(S["f_step"], 1)
            dve.wait_ge(S["f_act"], 2)
            dve.wait_ge(S["f_step"], 6)
            V.reciprocal(fw, fw).then_inc(S["f_step"], 1)
            TT(out=fx, in0=fx, in1=fl, op=ALU.subtract).then_inc(S["f_step"], 1)
            dve.wait_ge(S["f_step"], 8)
            TT(out=fe, in0=fe, in1=fw, op=ALU.mult).then_inc(S["f_step"], 1)
            dve.wait_ge(S["f_step"], 9)
            TT(out=fx, in0=fx, in1=fe, op=ALU.add).then_inc(S["f_step"], 1)
            dve.wait_ge(S["f_step"], 10)
            V.tensor_tensor_scan(out=fe, data0=fx, data1=fx, initial=0.0, op0=ALU.add, op1=ALU.bypass)\
                .then_inc(S["f_step"], 1)
            TS(F2[:, :], CS[:, :], 0.0, None, ALU.mult).then_inc(S["f2_set"], 1)
            for r in (0, 64):
                TT(out=PICK[r:r + DH2, :], in0=IDN[r:r + DH2, r:r + B2_HEADS],
                   in1=IDN[r:r + DH2, r + 32:r + 32 + B2_HEADS], op=ALU.add).then_inc(S["f2_set"], 1)

            def half_split(s, n, i=0):
                split_lo(dve, B2, s, (n,), i)

            def gating(h):
                tmp = (T0[:, :], U[:, 0:NT])[h % 2]
                b_s = ROWS[:, 2:3, h * P:(h + 1) * P].broadcast_to([P, QB, P])
                dve.wait_ge(S["sg_mm"], h + 1)
                if h == 0:
                    dve.wait_ge(S["ga_ev"], A_HEADS)
                    dve.wait_ge(S["f_step"], 11)
                else:
                    dve.wait_ge(S["sg_out"], h)
                TT(out=tmp.rearrange("p (t d) -> p t d", t=QB), in0=PS[2 + h % 2][:, :]
                   .rearrange("p (t d) -> p t d", t=QB), in1=b_s, op=ALU.add).then_inc(S["sg_tmp"], 1)
                dve.wait_ge(S["sg_tmp"], h + 1)
                TT(out=G[:, h, :], in0=G[:, h, :], in1=tmp, op=ALU.mult).then_inc(S["sg_out"], 1)

            def pair_out(p, b):
                g = feature(G[DH2 * b:DH2 * (b + 1)], 8 + p)
                dve.wait_ge(S["in2_ev"], T2_F + p + 1)
                dve.wait_ge(S["pv_mm"], QB * (HB + 2 * p + b + 1))
                TT(out=g, in0=PS[2][0:DH2, :], in1=g, op=ALU.mult).then_inc(S["pv_out"], 1)

            def pair(p, first):
                s, a, i = T2_PAIR, HB + 2 * p, 2 * p
                if not first:
                    pair_out(p - 1, 0)
                    row_max(a - 1, 3, 1.0)
                    recip(a - 1, 2)
                    pt_lo(a - 1, 0)
                    recip(a - 1, 3)
                    pt_lo(a - 1, 1)
                    pt_lo(a - 1, 2)
                    pt_lo(a - 1, 3)
                half_split(s + 2, 0, i)
                if not first:
                    pair_out(p - 1, 1)
                half_split(s + 2, 1, i)
                if first:
                    dve.wait_ge(S["f2_hi"], 2)
                    dve.wait_ge(S["f2_set"], 3)
                    for r in (32, 96):
                        TT(out=F2[r:r + 16, :], in0=fe, in1=F2[0:16, :].bitcast(F32), op=ALU.subtract)\
                            .then_inc(S["f2_set"], 1)
                    for h in range(4):
                        gating(h)
                    half_split(s + 3, 0, i)
                    for h in range(4, A_HEADS):
                        gating(h)
                dve.wait_ge(S["qn_hi"], HB + p + 1)
                STT(out=QNL[:, :], in0=PS[1][:, :], scalar=Q2_SCALE, in1=QNH[:, :].bitcast(F32), op0=ALU.mult,
                    op1=ALU.subtract).then_inc(S["qn_lo"], 1)
                if not first:
                    half_split(s + 3, 0, i)
                half_split(s + 3, 1, i)
                dve.wait_ge(S["kn_hi"], HB + p + 1)
                TT(out=KL[:, :], in0=PS[0][:, :], in1=KH[:, :].bitcast(F32), op=ALU.subtract).then_inc(S["kn_lo"], 1)
                row_max(a, 0, 1.0)
                row_max(a, 1, 1.0)
                recip(a, 0)
                half_split(s + 4, 0, i)
                row_max(a, 2, 1.0)
                recip(a, 1)
                row_max(a, 3, 1.0)
                recip(a, 2)
                recip(a, 3)
                half_split(s + 4, 1, i)
                pt_lo(a, 0)
                dve.wait_ge(S["v_hi"], HB + p + 1)
                TT(out=VSL[:, :, :], in0=PS[3][:, :].rearrange("p (t d) -> p t d", t=QB),
                   in1=VSH[:, :, :].bitcast(F32), op=ALU.subtract).then_inc(S["v_lo"], 1)
                pt_lo(a, 1)
                pt_lo(a, 2)
                pt_lo(a, 3)
                half_split(s + 5, 0, i)
                row_max(a + 1, 0, 1.0)
                row_max(a + 1, 1, 1.0)
                recip(a + 1, 0)
                half_split(s + 5, 1, i)
                row_max(a + 1, 2, 1.0)
                recip(a + 1, 1)

            pair(0, True)
            with dve.Fori(1, PAIRS) as p:
                pair(p, False)
            last = HB + B2_HEADS - 1

            def mix2_lo(k):
                dve.wait_ge(S["mix_hi"], KT * DEPTH + k + 1)
                TT(out=XL[:, k, :], in0=G[:, k, :], in1=XH[:, k, :].bitcast(F32), op=ALU.subtract)\
                    .then_inc(S["mix_lo"], 1)

            for k in range(3):
                mix2_lo(k)
            pair_out(PAIRS - 1, 0)
            row_max(last, 3, 1.0)
            recip(last, 2)
            recip(last, 3)
            for i in range(QB):
                for k in MIX_BEHIND[i]:
                    mix2_lo(k)
                pt_lo(last, i)
            half_split(T2_OUT + 2, 0)
            pair_out(PAIRS - 1, 1)
            mix2_lo(15)
            half_split(T2_OUT + 2, 1)
            def out_tile2(m, i=0):
                if m:
                    half_split(T2_OUT + m + 2, 0, i)
                dve.wait_ge(w_used, step_done(B2, T2_OUT + m, i))
                y = feature(Y, m + 2 * i)
                STT(out=y, in0=PS[(T2_OUT + m) % 2][:, :], scalar=column(MOD, 2 * KT + m + 2 * i), in1=y,
                    op0=ALU.mult, op1=ALU.add).then_inc(S["out2_ev"], 1)
                rms_sum(m + 2 * i)
                if m:
                    half_split(T2_OUT + m + 2, 1, i)

            out_tile2(0)
            out_tile2(1)
            with dve.Fori(0, KT // 2 - 2) as i:
                out_tile2(2, i)
                out_tile2(3, i)
            out_tile2(KT - 2)
            out_tile2(KT - 1)
            rms_end()
            for k in range(KT):
                STT(out=Y[:, k, :], in0=Y[:, k, :], scalar=EXT[:, E_FG + k:E_FG + k + 1], in1=PS[7][:, :],
                    op0=ALU.mult, op1=ALU.mult).then_inc(S["fin"], 1)

        @block.tensor
        def _(pe):
            mm = nc.tensor.matmul

            def column_sums(n):
                mm(PS[2][:, :], ONES[:, :], Y[:, 0, :], start=True, stop=True).then_inc(S["sh_mm"], 1)

            def norm_sums(n):
                pe.wait_ge(S["sum2"], KT * n)
                for a, acc in enumerate((A1, A2)):
                    for t in range(QB):
                        last = mm(PS[3][:, QB * a + t:QB * a + t + 1], acc[:, t * P:(t + 1) * P], ONES[:, 0:1],
                                  start=True, stop=True)
                last.then_inc(S["st_mm"], 1)
                for dg, s, bank, out in ((DG[0], S["dg_m"], 2, S["bc_m"]), (DG[1], S["dg_r"], 7, S["bc_r"])):
                    pe.wait_ge(s, QB * n)
                    for t in range(QB):
                        last = mm(PS[bank][:, t * P:(t + 1) * P], ONES[:, :], dg[:, t, :], start=True, stop=True)
                    last.then_inc(out, 1)

            pe.wait_ge(S["pool_set"], 5)
            pe.wait_ge(xt_in[0], 32)
            column_sums(0)
            for k in range(KT):
                pe.wait_ge(S["c_sq"], k + 1)
                mm(PS[7][:, :], ONES[:, :], SQ2[:, k, :], start=k == 0, stop=k == KT - 1)
            pe.wait_ge(S["emb_sum"], KT - 1)
            mm(PS[3][:, :], ONES[:, :], A1[:, :], start=True, stop=True).then_inc(S["emb_mm"], 1)

            def tile(l, s, bank, ready=None, order=range(KT), rows=P, mid={}, i=0):
                for n, k in enumerate(order):
                    half, col0 = n // 8, (n % 8) * P
                    slot, before, _ = unit(l, 2 * s + half, i)
                    if n % 8 == 0:
                        pe.wait_ge(w_lo, before + 1)
                    if ready:
                        pe.wait_ge(ready[0], ready[1] + n + 1)
                    last = products(PS[bank][:rows, :], WH[:, slot, col0:col0 + rows], WL[:, slot, col0:col0 + rows],
                                    XH[:, k, :], XL[:, k, :], n == 0, n == KT - 1)
                    if n % 8 == 7:
                        last.then_inc(w_used, 1)
                    for work in mid.get(n, ()):
                        work()
                return last

            def first_tiles(l):
                for k in range(KT):
                    half, col0 = k // 8, (k % 8) * P
                    if k % 8 == 0:
                        pe.wait_ge(w_lo, unit(l, 2 + half)[1] + 1)
                    pe.wait_ge(S["x_lo_s"], KT * l + k + 1)
                    for t in range(2):
                        slot = unit(l, 2 * t + half)[0]
                        last = products(PS[t][:, :], WH[:, slot, col0:col0 + P], WL[:, slot, col0:col0 + P],
                                        XH[:, k, :], XL[:, k, :], k == 0, k == KT - 1)
                        if k == KT - 1:
                            last.then_inc(w_used, 1 + t)
                    if k == 7:
                        last.then_inc(w_used, 1)

            def layer(l):

                def in_tile(m, mid={}, i=0):
                    if m != T_KR:
                        pe.wait_ge(S["in_ev"], taken(l, m - 2) + 2 * i)
                    tile(l, m, m % 2 if m != T_KR else 7, rows=P if m != T_KR else ROPE, mid=mid, i=i)

                def pool_mm(j):
                    pe.wait_ge(S["pool_step"], 32 * l + (5, 12, 21, 32)[j])
                    pe.wait_ge(S["pool_ev"], GROUPS * l + j)
                    if j == 0:
                        pe.wait_ge(S["wpool_in"], 16 * (l + 1))
                    mm(PS[4][:, :], WP[:, j, :], ((U, Y1)[j % 2])[:, 0:NT], start=True, stop=True)\
                        .then_inc(S["pool_mm"], 1)

                def lat_sums(q):
                    n = 2 * l + q
                    pe.wait_ge(S["sq_sum"], 4 * l + (1, 4)[q])
                    for t in range(QB):
                        last = mm(PS[5][:, t:t + 1], T0[:, t * P:(t + 1) * P], ONES[:, 0:1], start=True, stop=True)
                    last.then_inc(S["lat_mm"], 1)

                def lat_bcast(q):
                    n = 2 * l + q
                    pe.wait_ge(S["lat_dg"], QB * (n + 1))
                    for t in range(QB):
                        last = mm(PS[6][:, t * P:(t + 1) * P], ONES[:, :], T0[:, t * P:(t + 1) * P],
                                  start=True, stop=True)
                    last.then_inc(S["lat_bc"], 1)

                first_tiles(l)
                for m in range(2, T_CONV + 1):
                    in_tile(m, {T_Q: {7: [lambda: lat_sums(0)]}, T_Q + 1: {2: [lambda: lat_bcast(0)]},
                                T_KR: {7: [lambda: lat_sums(1)]}, T_KR + 1: {2: [lambda: lat_bcast(1)]}}.get(m, {}))
                    if m in range(T_POOL + 2, T_CONV + 1, 2):
                        pool_mm((m - T_POOL - 2) // 2)
                with pe.Fori(0, (IN_TILES - T_CONV - 1) // 2) as i:
                    in_tile(T_CONV + 1, i=i)
                    in_tile(T_CONV + 2, i=i)
                in_tile(IN_TILES - 1)

                def head_proj(h):
                    hh = HEADS * l + h
                    kv_slot, before, _ = unit(l, POS_HEAD + 2 * h)
                    q_slot = unit(l, POS_HEAD + 2 * h + 1)[0]

                    def project(out, slot, cols, k0, kt, wide=P):
                        for k in range(kt):
                            if h == 0:
                                pe.wait_ge(S["lat_lo"], 6 * l + k0 + k - 7)
                            c = cols + k * wide
                            last = products(out, WH[:, slot, c:c + wide], WL[:, slot, c:c + wide],
                                            XH[:, k0 + k, :], XL[:, k0 + k, :], k == 0, k == kt - 1)
                        return last

                    def pv1(i):
                        if i == 0:
                            pe.wait_ge(S["kn_lo"], hh + 1)
                        pv(hh - 1, i, PS[2], slice(0, VDIM), hh)

                    pe.wait_ge(w_lo, before + 2)
                    if h == 0:
                        pe.wait_ge(S["in_ev"], taken(l, IN_TILES - 2))
                    pe.wait_ge(S["rope_q"], 5 * hh)
                    project(PS[1][0:ROPE, :], q_slot, 0, 8, 4, ROPE).then_inc(S["proj"], 1)
                    pe.wait_ge(S["pv_out"], max(hh - 1, 0))
                    project(PS[2][:, :], kv_slot, 0, 12, 2).then_inc(S["proj"], 1)
                    if h:
                        trans(hh - 1, 0)
                    pe.wait_ge(S["v_lo"], hh)
                    for t in range(QB):
                        tok = slice(t * P, (t + 1) * P)
                        for k in range(2):
                            c = (2 + k) * P
                            last = products(PS[3][:, tok], XH[:, 12 + k, tok], XL[:, 12 + k, tok],
                                            WH[:, kv_slot, c:c + P], WL[:, kv_slot, c:c + P], k == 0, k == 1)
                    last.then_inc(w_used, 1)
                    if h:
                        trans(hh - 1, 1)
                        pv1(0)
                        trans(hh - 1, 2)
                    pe.wait_ge(S["qn_lo"], hh)
                    pe.wait_ge(S["in_ev"], EV_TILES * (l + 1))
                    project(PS[0][:, :], q_slot, 4 * ROPE, 8, 4).then_inc(w_used, 1)
                    if h:
                        pv1(1)
                        trans(hh - 1, 3)
                        pv1(2)
                        pv1(3)

                def scores(hh, i):
                    bank, n = 5 - i % 2, P * (i + 1)
                    if i == 0:
                        for s, v in (("kn_lo", hh + 1), ("qn_lo", hh + 1), ("rope_q", 5 * hh + 5), ("krl", l + 1)):
                            pe.wait_ge(S[s], v)
                        pe.wait_ge(S["krh"], 8 * (l + 1))
                    pe.wait_ge(S["s_exp"], QB * hh + max(i - 1, 0))
                    q = slice(i * P, (i + 1) * P)
                    out = PS[bank][:, 0:n]
                    mm(out, QNH[:, q], XL[:, 15, 0:n], start=True, stop=False)
                    mm(out, QNL[:, q], XH[:, 15, 0:n], start=False, stop=False)
                    mm(out, QNH[:, q], XH[:, 15, 0:n], start=False, stop=False)
                    mm(out, QR[:, q], XH[:, 14, 0:n], start=False, stop=False)
                    mm(out, QR[0:ROPE, q], XL[0:ROPE, 14, 0:n], start=False, stop=False)
                    mm(PS[bank][:, n - P:n], IDB, MASK[:, :], start=False, stop=True).then_inc(S["s_mm"], 1)

                for h in range(HEADS):
                    head_proj(h)
                    for i in range(QB):
                        scores(HEADS * l + h, i)
                last = HEADS * (l + 1) - 1

                def tr(i):
                    return lambda: trans(last, i)

                def pr(i):
                    return lambda: pv(last, i, PS[2], slice(0, VDIM), last + 1)

                tile(l, T_OUT, 0, (S["mix_lo"], KT * l), MIX_ORDER,
                     mid={0: [tr(0)], 1: [tr(1)], 3: [pr(0), tr(2)], 5: [pr(1), tr(3)], 7: [pr(2)], 9: [pr(3)]})
                tile(l, T_OUT + 1, 1, order=MIX_ORDER)
                pe.wait_ge(S["out_ev"], KT * l + 1)
                column_sums(l + 1)
                with pe.Fori(0, KT // 2 - 1) as i:
                    for m in (2, 3):
                        pe.wait_ge(S["out_ev"], KT * l + m - 1 + 2 * i)
                        tile(l, T_OUT + m, m % 2, order=MIX_ORDER, i=i)
                norm_sums(l + 1)

            def trans(hh, i):
                pe.wait_ge(S["p_norm"], QB * hh + i + 1)
                pe.wait_ge(S["pt_lo"], QB * hh + max(i - 1, 0))
                for j in range(i + 1):
                    last = nc.tensor.transpose(PS[6 + i % 2][:, j * P:(j + 1) * P],
                                               PR[:, poff(i) + j * P:poff(i) + (j + 1) * P], IDN[:, :])
                last.then_inc(S["p_tr"], 1)

            def pv(hh, i, out, vcols, v_ready):
                pe.wait_ge(S["pt_lo"], QB * hh + i + 1)
                if i == 0:
                    pe.wait_ge(S["v_lo"], v_ready)
                    pe.wait_ge(S["pv_out"], hh)
                for j in range(i + 1):
                    c = slice(j * P, (j + 1) * P)
                    last = products(out[:, i * P:(i + 1) * P], VSH[:, j, vcols], VSL[:, j, vcols],
                                    PTH[i % 2][:, c], PTL[i % 2][:, c], j == 0, j == i)
                last.then_inc(S["pv_mm"], 1)

            for l in range(DEPTH):
                layer(l)

            def rms_sums():
                pe.wait_ge(S["r_sum"], KT)
                for t in range(QB):
                    last = mm(PS[3][:, t:t + 1], A1[:, t * P:(t + 1) * P], ONES[:, 0:1], start=True, stop=True)
                last.then_inc(S["r_mm"], 1)
                pe.wait_ge(S["r_dg"], QB)
                for t in range(QB):
                    last = mm(PS[7][:, t * P:(t + 1) * P], ONES[:, :], DG[1][:, t, :], start=True, stop=True)
                last.then_inc(S["r_bc"], 1)

            def va_trans(j):
                pe.wait_ge(S["in2_ev"], T2_VA + j + 1)
                pe.wait_ge(S["va_ev"], max(j - 1, 0))
                buf = (T0, Y1)[j % 2]
                for t in range(QB):
                    last = nc.tensor.transpose(PS[2 + j % 2][:, t * P:(t + 1) * P], buf[:, t * P:(t + 1) * P],
                                               IDN[:, :])
                last.then_inc(S["va_tr"], 1)

            def spatial(h):
                pe.wait_ge(S["sg_v"], QB)
                pe.wait_ge(S["ws_set"], 1)
                pe.wait_ge(S["sg_tmp"], max(h - 1, 0))
                for t in range(QB):
                    last = mm(PS[2 + h % 2][:, t * P:(t + 1) * P], VA[:, t, h * P:(h + 1) * P], WST[:, h, :],
                              start=True, stop=True)
                last.then_inc(S["sg_mm"], 1)

            def scores2(p, b, i):
                bank, n, hh = 5 - i % 2, P * (i + 1), HB + 2 * p + b
                if i == 0:
                    pe.wait_ge(S["kn_lo"], HB + p + 1)
                    pe.wait_ge(S["qn_lo"], HB + p + 1)
                    pe.wait_ge(S["f2_set"], 5)
                    pe.wait_ge(S["npick"], 2 * (2 * p + b + 1))
                pe.wait_ge(S["s_exp"], QB * hh + max(i - 1, 0))
                q, r = slice(i * P, (i + 1) * P), slice(DH2 * b, DH2 * (b + 1))
                out = PS[bank][:, 0:n]
                mm(out, QNH[r, q], KL[r, 0:n], start=True, stop=False)
                mm(out, QNL[r, q], KH[r, 0:n], start=False, stop=False)
                mm(out, QNH[r, q], KH[r, 0:n], start=False, stop=False)
                mm(out, NPICK[b][r, :], F2[r, 0:n], start=False, stop=False)
                pick = PPICK[b][r, 0:2].rearrange("p (a b) -> p a b", a=1).broadcast_to([DH2, n // 2, 2])
                mm(out, F2[r, q], pick, start=False, stop=False)
                mm(PS[bank][:, n - P:n], IDB, MASK[:, :], start=False, stop=True).then_inc(S["s_mm"], 1)

            def pv2(p, b, i):
                pv(HB + 2 * p + b, i, PS[2][0:DH2, :], slice(DH2 * b, DH2 * (b + 1)), HB + p + 1)

            def trans2(p, b, i):
                trans(HB + 2 * p + b, i)

            def v_transpose2(p):
                pe.wait_ge(S["v_out"], p + 1)
                pe.wait_ge(S["v_lo"], HB + p)
                for t in range(QB):
                    last = nc.tensor.transpose(PS[3][:, t * P:(t + 1) * P], TV[:, t * P:(t + 1) * P], IDN[:, :])
                last.then_inc(S["v_tr"], 1)

            for k in range(KT):
                pe.wait_ge(S["r_sq"], k + 1)
                last = mm(PS[6][:, :], ONES[:, :], SQ2[:, k, :], start=k == 0, stop=k == KT - 1)
            last.then_inc(S["r_mm"], 1)
            first_tiles(B2)
            for s in range(2, T2_U + 2):
                pe.wait_ge(S["in2_ev"], s - 1)
                tile(B2, s, s % 2, mid={1: [lambda: va_trans(0)] if s == 2 else [],
                                        5: [lambda: va_trans(s - 1)] if s <= T2_U else []})
            with pe.Fori(0, (T2_F - T2_U) // 2 - 1) as i:
                for s in (T2_U + 2, T2_U + 3):
                    pe.wait_ge(S["in2_ev"], s - 1 + 2 * i)
                    tile(B2, s, s % 2, i=i)
            tile(B2, T2_F, 6, rows=B2_HEADS)

            def do(f, *x):
                return lambda: f(*x)

            def second_half(p):
                return {0: [do(scores2, p, 1, 3)], 2: [do(trans2, p, 1, 0)], 4: [do(trans2, p, 1, 1)],
                        7: [do(pv2, p, 1, 0), do(trans2, p, 1, 2)], 9: [do(pv2, p, 1, 1), do(trans2, p, 1, 3)],
                        11: [do(pv2, p, 1, 2)], 13: [do(pv2, p, 1, 3)]}

            def pair(p, first):
                s, i = T2_PAIR, 2 * p
                if first:
                    pe.wait_ge(S["in2_ev"], T2_F)
                else:
                    pe.wait_ge(S["v_out"], p)
                tile(B2, s, 1, mid={} if first else second_half(p - 1), i=i)
                pe.wait_ge(S["in2_ev"], T2_F + p)
                tile(B2, s + 1, 0, mid={2 * h: [do(spatial, h)] for h in range(A_HEADS)} if first else {}, i=i)
                pe.wait_ge(S["qn_lo"], HB + p + 1)
                tile(B2, s + 2, 1, mid={4 + 3 * q: [do(scores2, p, 0, q)] for q in range(QB)}, i=i)
                pe.wait_ge(S["kn_lo"], HB + p + 1)
                tile(B2, s + 3, 0, mid={
                    0: [do(trans2, p, 0, 0)], 2: [do(v_transpose2, p), do(trans2, p, 0, 1)],
                    5: [do(pv2, p, 0, 0), do(trans2, p, 0, 2)], 7: [do(pv2, p, 0, 1), do(trans2, p, 0, 3)],
                    9: [do(pv2, p, 0, 2)], 11: [do(pv2, p, 0, 3), do(scores2, p, 1, 0)],
                    13: [do(scores2, p, 1, 1)], 15: [do(scores2, p, 1, 2)]}, i=i)

            pair(0, True)
            with pe.Fori(1, PAIRS) as p:
                pair(p, False)
            pe.wait_ge(S["v_out"], PAIRS)
            behind = second_half(PAIRS - 1)
            for work in behind.pop(0):
                work()
            tile(B2, T2_OUT, T2_OUT % 2, (S["mix_lo"], KT * DEPTH), mid=behind)
            pe.wait_ge(S["in2_ev"], T2_F + PAIRS)
            tile(B2, T2_OUT + 1, (T2_OUT + 1) % 2)
            with pe.Fori(0, KT // 2 - 1) as i:
                for m in (2, 3):
                    pe.wait_ge(S["out2_ev"], m - 1 + 2 * i)
                    tile(B2, T2_OUT + m, (T2_OUT + m) % 2, i=i)
            rms_sums()


IN_COLS = {"q": 0, "kv": 512, "kr": 768, "g_mla": 832, "p_in": 1856, "g_pool": 2368,
           "c_h": 2880, "c_b": 3392, "c_c": 3904, "g_conv": 4416}


def in_tiles():
    c = IN_COLS
    out = [c["kv"] + P * i for i in range(2)] + [c["q"] + P * i for i in range(4)] + [c["kr"]]
    for j in range(GROUPS):
        out += [c["g_pool"] + P * j, c["p_in"] + P * j]
    for j in range(GROUPS):
        out += [c[n] + P * j for n in ("c_h", "c_c", "c_b", "g_conv")]
    out += [c["g_mla"] + P * m for m in range(8)]
    return out


IN_COLS_2 = {"u": 0, "v": 1024, "g_a": 2048, "q": 3072, "k": 4096, "v_b": 5120, "g_b": 6144, "f": 7168}


def tile_units(w, c0, cols=P, order=None):
    t = np.zeros((P, KT, P), w.dtype)
    t[:, :, :cols] = w[:, c0:c0 + cols].reshape(KT, P, cols)[list(order or range(KT))].transpose(1, 0, 2)
    return [t[:, :8].reshape(P, UNIT), t[:, 8:].reshape(P, UNIT)]


def pack_stream(w_in, w_uq, w_ukv, w_out):
    units = []
    for l in range(DEPTH):
        for c0 in in_tiles():
            units += tile_units(w_in[l], c0, ROPE if c0 == IN_COLS["kr"] else P)
        uq = w_uq[l].reshape(4, P, HEADS, NOPE + ROPE)
        ukv = w_ukv[l].reshape(2, P, HEADS, NOPE + VDIM)
        for h in range(HEADS):
            kv, q = np.zeros((P, UNIT), w_in.dtype), np.zeros((P, UNIT), w_in.dtype)
            kv[:, :256] = ukv[:, :, h, :NOPE].transpose(1, 0, 2).reshape(P, 256)
            kv[:, 256:512] = ukv[:, :, h, NOPE:].transpose(1, 0, 2).reshape(P, 256)
            q[:, :256] = uq[:, :, h, NOPE:].transpose(1, 0, 2).reshape(P, 256)
            q[:, 256:768] = uq[:, :, h, :NOPE].transpose(1, 0, 2).reshape(P, 512)
            units += [kv, q]
        for m in range(KT):
            units += tile_units(w_out[l], P * m, order=MIX_ORDER)
    return units


def pack_stream_2(w_in, w_out):
    c = IN_COLS_2
    units = []
    for part in ("v", "u", "g_a"):
        for m in range(8):
            units += tile_units(w_in, c[part] + P * m)
    units += tile_units(w_in, c["f"], B2_HEADS)
    for p in range(PAIRS):
        for part in ("q", "k", "v_b", "g_b"):
            units += tile_units(w_in, c[part] + P * p)
    for m in range(KT):
        units += tile_units(w_out, P * m)
    return units


def columns(v):
    v = np.asarray(v)
    return v.reshape(-1, P).T


def kernel(**inputs):
    import concourse.bacc as bacc
    from concourse.bass_utils import run_bass_kernel_spmd

    a = {k: np.asarray(v) for k, v in inputs.items()}
    f32 = np.float32
    stream = np.stack(pack_stream(a["w_in"], a["w_uq"], a["w_ukv"], a["w_out"])
                      + pack_stream_2(a["w_in_2"][0], a["w_out_2"][0]))
    layers = np.concatenate([np.concatenate([
        columns(a["q_norm_g"][l]), columns(a["kv_norm_g"][l]), columns(a["pool_scale"][l]),
        a["conv_w"][l].reshape(TAPS, GROUPS, P).transpose(2, 1, 0).reshape(P, GROUPS * TAPS),
        columns(a["b_out"][l]), columns(a["ln_g"][l]), columns(a["ln_b"][l])], 1) for l in range(DEPTH)], 1)
    b_f = np.zeros((P, 1), f32)
    b_f[:B2_HEADS, 0] = a["b_f_2"][0]
    extra = np.concatenate([columns(a[n]) for n in ("emb_ln_g", "emb_ln_b", "norm_g_2", "final_g_2", "b_ada_2")]
                           + [b_f], 1)
    half = ROPE // 2
    freq = (10000.0 ** (-np.arange(half, dtype=f32) / half)).astype(f32)
    row = np.arange(P)
    phase = np.where(row < 64, np.pi / 2, np.where(row < 96, 0.0, np.pi))
    invf = np.stack([freq[row % half], phase / TWO_PI, phase], 1).astype(f32)
    arrays = {
        "layers": layers, "extra": extra, "stream": stream,
        "wada": a["w_ada_2"][0].T.reshape(ADA_TILES, P, 2, UNIT).transpose(0, 2, 1, 3)
        .reshape(ADA_UNITS, P, UNIT),
        "wsT": a["w_s_2"][0].transpose(2, 0, 1),
        "wpool": a["w_pool"].transpose(0, 2, 1, 3), "cond": a["c_2"].reshape(1, D),
        "rows": np.stack([a["ln_v_g_2"][0], a["ln_v_b_2"][0], a["b_s_2"][0].reshape(WIDTH_A)])[None],
        "positions": a["positions"].reshape(1, NT), "invf": invf,
        "xT": a["x"][0].T.reshape(KT, P, NT),
    }
    nc = bacc.Bacc("TRN2", target_bir_lowering=False, num_devices=1)
    aps = {}
    for name in list(arrays):
        arrays[name] = np.ascontiguousarray(arrays[name])
        aps[name] = nc.dram_tensor(name, arrays[name].shape, mybir.dt.from_np(arrays[name].dtype),
                                   kind="ExternalInput").ap()
    aps["outT"] = nc.dram_tensor("outT", (KT, P, NT), F32, kind="ExternalOutput").ap()
    build(nc, **aps)
    r = run_bass_kernel_spmd(nc, [arrays], core_ids=[0])
    return r.results[0]["outT"].reshape(D, NT).T[None]
```
